# Optimizing a Trainium2 kernel written in Bass

```python
import math
import jax
import jax.numpy as jnp
from jax import lax
import numpy as np
import jax, jax.numpy as jnp

D_MODEL = 1024
BATCH = 1
SEQ = 256
DEPTH = 2

CHUNK = 64
Q_BLOCK = 128
HEAD_DIM = 64
ROPE_DIM = HEAD_DIM // 4
ROPE_THETA = 500000.0
RMS_EPS = 1e-6
A_HEADS = D_MODEL // (2 * HEAD_DIM)
A_WIDTH = A_HEADS * HEAD_DIM
B_HEADS = D_MODEL // (4 * HEAD_DIM)
B_QK_WIDTH = B_HEADS * 2 * HEAD_DIM
B_VDIM = 2 * HEAD_DIM
B_WIDTH = B_HEADS * B_VDIM
C_WIDTH = D_MODEL // 2
CONV_W = 3
D_HEADS = D_MODEL // (2 * HEAD_DIM)
D_WIDTH = D_HEADS * HEAD_DIM
D_LEFT_CHUNKS = 8
D_BAND = (D_LEFT_CHUNKS + 1) * CHUNK
REL_CLIP = 128
X_HEADS = 4
X_HEAD_DIM = D_MODEL // X_HEADS
N_MEM = 256
D_FF = 2816
N_EVEN = (DEPTH + 1) // 2
N_ODD = DEPTH // 2
EVEN_SIZES = (A_WIDTH, A_WIDTH, A_WIDTH, A_HEADS, B_QK_WIDTH, B_QK_WIDTH, B_WIDTH)
ODD_SIZES = (C_WIDTH, C_WIDTH, C_WIDTH, D_WIDTH, D_WIDTH, D_WIDTH)
EVEN_IN = 3 * A_WIDTH + A_HEADS + 2 * B_QK_WIDTH + B_WIDTH
ODD_IN = 3 * C_WIDTH + 3 * D_WIDTH
EVEN_MIX = A_WIDTH + B_WIDTH
ODD_MIX = C_WIDTH + D_WIDTH
MAX_POS_OFFSET = 65536


def rms_norm(x, g):
    xf = x.astype(jnp.float32)
    y = xf * lax.rsqrt(jnp.mean(xf * xf, axis=-1, keepdims=True) + RMS_EPS)
    return (y * g.astype(jnp.float32)).astype(x.dtype)

def split_cols(y, sizes):
    out, start = [], 0
    for s in sizes:
        out.append(y[..., start:start + s])
        start += s
    return out

def rope_tables(positions):
    inv = ROPE_THETA ** (-jnp.arange(0, ROPE_DIM, 2, dtype=jnp.float32) / ROPE_DIM)
    ang = positions.astype(jnp.float32)[..., None] * inv
    return jnp.cos(ang), jnp.sin(ang)

def apply_partial_rope(x, cos, sin):
    half = ROPE_DIM // 2
    bshape = cos.shape[:2] + (1,) * (x.ndim - 3) + (half,)
    c, s = cos.reshape(bshape), sin.reshape(bshape)
    xr = x[..., :ROPE_DIM].astype(jnp.float32)
    x1, x2 = xr[..., :half], xr[..., half:]
    rot = jnp.concatenate([x1 * c - x2 * s, x2 * c + x1 * s], axis=-1).astype(x.dtype)
    return jnp.concatenate([rot, x[..., ROPE_DIM:]], axis=-1)

def swiglu(h, w_in, w_out):
    g, u = split_cols(h @ w_in, (D_FF, D_FF))
    return (jax.nn.silu(g) * u) @ w_out

def forgetting_attention(q, k, v, cum_logf):
    seq = q.shape[1]
    scale = q.shape[-1] ** -0.5
    outs = []
    for qs in range(0, seq, Q_BLOCK):
        qe = qs + Q_BLOCK
        s = jnp.einsum('bqhd,bkhd->bhqk', q[:, qs:qe], k[:, :qe],
                       preferred_element_type=jnp.float32) * scale
        s = s + cum_logf[:, :, qs:qe, None] - cum_logf[:, :, None, :qe]
        causal = jnp.arange(qs, qe)[:, None] >= jnp.arange(qe)[None, :]
        p = jax.nn.softmax(jnp.where(causal, s, -jnp.inf), axis=-1).astype(v.dtype)
        outs.append(jnp.einsum('bhqk,bkhd->bqhd', p, v[:, :qe]))
    return jnp.concatenate(outs, axis=1)

def differential_attention(q, k, v, lam):
    seq = q.shape[1]
    scale = q.shape[-1] ** -0.5
    outs = []
    for qs in range(0, seq, Q_BLOCK):
        qe = qs + Q_BLOCK
        s = jnp.einsum('bqhjd,bkhjd->bhjqk', q[:, qs:qe], k[:, :qe],
                       preferred_element_type=jnp.float32) * scale
        allowed = (jnp.arange(qs, qe)[:, None] // CHUNK) >= (jnp.arange(qe)[None, :] // CHUNK)
        p = jax.nn.softmax(jnp.where(allowed, s, -jnp.inf), axis=-1)
        p = (p[:, :, 0] - lam * p[:, :, 1]).astype(v.dtype)
        outs.append(jnp.einsum('bhqk,bkhe->bqhe', p, v[:, :qe]))
    return jnp.concatenate(outs, axis=1)

def short_conv_mixer(gate_b, gate_c, h, conv_w):
    u = gate_c * h
    y = lax.conv_general_dilated(u, conv_w[:, None, :], window_strides=(1,),
                                 padding=[(CONV_W - 1, 0)],
                                 dimension_numbers=('NWC', 'WIO', 'NWC'),
                                 feature_group_count=u.shape[-1])
    return gate_b * y

def chunk_band_attention(q, k, v, rel_table):
    bsz, seq, heads, hd = q.shape
    n_chunks = seq // CHUNK
    left = D_LEFT_CHUNKS * CHUNK
    pad = ((0, 0), (left, 0), (0, 0), (0, 0))
    kp, vp = jnp.pad(k, pad), jnp.pad(v, pad)
    rel = jnp.arange(CHUNK)[:, None] - jnp.arange(D_BAND)[None, :] + left
    rel_idx = jnp.clip(rel, -REL_CLIP, REL_CLIP) + REL_CLIP
    bias = rel_table[:, rel_idx].astype(jnp.float32)
    scale = hd ** -0.5

    def one_chunk(c):
        start = c * CHUNK
        qc = lax.dynamic_slice_in_dim(q, start, CHUNK, axis=1)
        kc = lax.dynamic_slice_in_dim(kp, start, D_BAND, axis=1)
        vc = lax.dynamic_slice_in_dim(vp, start, D_BAND, axis=1)
        s = jnp.einsum('bqhd,bkhd->bhqk', qc, kc, preferred_element_type=jnp.float32) * scale + bias
        valid = (start - left + jnp.arange(D_BAND)) >= 0
        p = jax.nn.softmax(jnp.where(valid, s, -jnp.inf), axis=-1).astype(v.dtype)
        return jnp.einsum('bhqk,bkhd->bqhd', p, vc)

    out = lax.map(one_chunk, jnp.arange(n_chunks))
    return out.transpose(1, 0, 2, 3, 4).reshape(bsz, seq, heads * hd)

def even_mixer(h, w_in, f_bias, qk_gains, lam_params, subln_gain, lambda_init, w_out, cos, sin):
    bsz, seq, _ = h.shape
    a_q, a_k, a_v, a_f, b_q, b_k, b_v = split_cols(h @ w_in, EVEN_SIZES)
    aq = rms_norm(a_q.reshape(bsz, seq, A_HEADS, HEAD_DIM), qk_gains[0])
    ak = rms_norm(a_k.reshape(bsz, seq, A_HEADS, HEAD_DIM), qk_gains[1])
    av = a_v.reshape(bsz, seq, A_HEADS, HEAD_DIM)
    logf = jax.nn.log_sigmoid((a_f + f_bias).astype(jnp.float32))
    cum_logf = jnp.cumsum(logf, axis=1).transpose(0, 2, 1)
    a_out = forgetting_attention(aq, ak, av, cum_logf).reshape(bsz, seq, A_WIDTH)
    bq = rms_norm(b_q.reshape(bsz, seq, B_HEADS, 2, HEAD_DIM), qk_gains[2])
    bk = rms_norm(b_k.reshape(bsz, seq, B_HEADS, 2, HEAD_DIM), qk_gains[3])
    bq, bk = apply_partial_rope(bq, cos, sin), apply_partial_rope(bk, cos, sin)
    bv = b_v.reshape(bsz, seq, B_HEADS, B_VDIM)
    lp = lam_params.astype(jnp.float32)
    lam = jnp.exp(jnp.sum(lp[0] * lp[1])) - jnp.exp(jnp.sum(lp[2] * lp[3])) + lambda_init
    b_out = differential_attention(bq, bk, bv, lam)
    b_out = (rms_norm(b_out, subln_gain) * (1.0 - lambda_init)).reshape(bsz, seq, B_WIDTH)
    return jnp.concatenate([a_out, b_out], axis=-1) @ w_out

def odd_mixer(h, w_in, conv_w, qk_gains, rel_table, w_out):
    bsz, seq, _ = h.shape
    c_b, c_c, c_h, d_q, d_k, d_v = split_cols(h @ w_in, ODD_SIZES)
    c_out = short_conv_mixer(c_b, c_c, c_h, conv_w)
    dq = rms_norm(d_q.reshape(bsz, seq, D_HEADS, HEAD_DIM), qk_gains[0])
    dk = rms_norm(d_k.reshape(bsz, seq, D_HEADS, HEAD_DIM), qk_gains[1])
    dv = d_v.reshape(bsz, seq, D_HEADS, HEAD_DIM)
    d_out = chunk_band_attention(dq, dk, dv, rel_table)
    return jnp.concatenate([c_out, d_out], axis=-1) @ w_out

def memory_cross_attention(h, mem_n, w_q, w_kv, qk_gains, w_o):
    bsz, seq, _ = h.shape
    q = rms_norm((h @ w_q).reshape(bsz, seq, X_HEADS, X_HEAD_DIM), qk_gains[0])
    k, v = split_cols(mem_n @ w_kv, (D_MODEL, D_MODEL))
    k = rms_norm(k.reshape(bsz, -1, X_HEADS, X_HEAD_DIM), qk_gains[1])
    v = v.reshape(bsz, -1, X_HEADS, X_HEAD_DIM)
    s = jnp.einsum('bqhd,bkhd->bhqk', q, k, preferred_element_type=jnp.float32) * X_HEAD_DIM ** -0.5
    p = jax.nn.softmax(s, axis=-1).astype(v.dtype)
    o = jnp.einsum('bhqk,bkhd->bqhd', p, v).reshape(bsz, seq, D_MODEL)
    return o @ w_o

def first_inputs(seed: int = 0) -> dict:
    key = jax.random.key(seed)
    ks = jax.random.split(key, 24)
    f32 = jnp.float32

    def dense(k, shape):
        return jax.random.normal(k, shape, f32) * shape[-2] ** -0.5

    def gain(k, shape):
        return 1.0 + 0.05 * jax.random.normal(k, shape, f32)

    x = jax.random.normal(ks[0], (BATCH, SEQ, D_MODEL), f32)
    mem = jax.random.normal(ks[1], (BATCH, N_MEM, D_MODEL), f32)
    offset = jax.random.randint(ks[2], (BATCH, 1), 0, MAX_POS_OFFSET, dtype=jnp.int32)
    positions = offset + jnp.arange(SEQ, dtype=jnp.int32)[None, :]
    return {
        'x': x,
        'mem': mem,
        'positions': positions,
        'ln_gains': gain(ks[3], (DEPTH, 5, D_MODEL)),
        'ffn1_w_in': dense(ks[4], (DEPTH, D_MODEL, 2 * D_FF)),
        'ffn1_w_out': dense(ks[5], (DEPTH, D_FF, D_MODEL)),
        'ffn2_w_in': dense(ks[6], (DEPTH, D_MODEL, 2 * D_FF)),
        'ffn2_w_out': dense(ks[7], (DEPTH, D_FF, D_MODEL)),
        'even_w_in': dense(ks[8], (N_EVEN, D_MODEL, EVEN_IN)),
        'even_f_bias': jax.random.uniform(ks[9], (N_EVEN, A_HEADS), f32, 1.0, 5.0),
        'even_qk_gains': gain(ks[10], (N_EVEN, 4, HEAD_DIM)),
        'even_lambda': 0.1 * jax.random.normal(ks[11], (N_EVEN, 4, HEAD_DIM), f32),
        'even_subln_gain': gain(ks[12], (N_EVEN, B_VDIM)),
        'even_w_out': dense(ks[13], (N_EVEN, EVEN_MIX, D_MODEL)),
        'odd_w_in': dense(ks[14], (N_ODD, D_MODEL, ODD_IN)),
        'odd_conv_w': jax.random.normal(ks[15], (N_ODD, CONV_W, C_WIDTH), f32) * CONV_W ** -0.5,
        'odd_qk_gains': gain(ks[16], (N_ODD, 2, HEAD_DIM)),
        'odd_rel_bias': 0.5 * jax.random.normal(ks[17], (N_ODD, D_HEADS, 2 * REL_CLIP + 1), f32),
        'odd_w_out': dense(ks[18], (N_ODD, ODD_MIX, D_MODEL)),
        'x_w_q': dense(ks[19], (DEPTH, D_MODEL, D_MODEL)),
        'x_w_kv': dense(ks[20], (DEPTH, D_MODEL, 2 * D_MODEL)),
        'x_qk_gains': gain(ks[21], (DEPTH, 2, X_HEAD_DIM)),
        'x_w_o': dense(ks[22], (DEPTH, D_MODEL, D_MODEL)),
    }

def first_block(x, mem, positions, ln_gains, ffn1_w_in, ffn1_w_out, ffn2_w_in, ffn2_w_out,
              even_w_in, even_f_bias, even_qk_gains, even_lambda, even_subln_gain, even_w_out,
              odd_w_in, odd_conv_w, odd_qk_gains, odd_rel_bias, odd_w_out,
              x_w_q, x_w_kv, x_qk_gains, x_w_o):
    cos, sin = rope_tables(positions)
    for layer in range(DEPTH):
        g = ln_gains[layer]
        x = x + 0.5 * swiglu(rms_norm(x, g[0]), ffn1_w_in[layer], ffn1_w_out[layer])
        h = rms_norm(x, g[1])
        if layer % 2 == 0:
            e = layer // 2
            lambda_init = 0.8 - 0.6 * math.exp(-0.3 * layer)
            mixed = even_mixer(h, even_w_in[e], even_f_bias[e], even_qk_gains[e], even_lambda[e],
                               even_subln_gain[e], lambda_init, even_w_out[e], cos, sin)
        else:
            o = layer // 2
            mixed = odd_mixer(h, odd_w_in[o], odd_conv_w[o], odd_qk_gains[o], odd_rel_bias[o],
                              odd_w_out[o])
        x = x + mixed
        x = x + memory_cross_attention(rms_norm(x, g[2]), rms_norm(mem, g[3]), x_w_q[layer],
                                       x_w_kv[layer], x_qk_gains[layer], x_w_o[layer])
        x = x + 0.5 * swiglu(rms_norm(x, g[4]), ffn2_w_in[layer], ffn2_w_out[layer])
    return x


RET_HEADS = 4
RET_DK = 128
RET_DV = 128
RET_CHUNK = 128
RET_THETA = 10000.0
DIL_HEADS = 8
DIL_DH = 64
DIL_PATTERNS = ((128, 1), (512, 4), (2048, 16))
DIL_BLOCK = 128
ROT_DIM = DIL_DH // 4
GLA_HEADS = 4
GLA_DK = (D_MODEL // 2) // GLA_HEADS
GLA_DV = D_MODEL // GLA_HEADS
GLA_LOWRANK = 16
GLA_TAU = 16.0
GLA_CHUNK = 64
FFN_HIDDEN = 2816
EPS = 1e-6

EVEN_SIZES_2 = (RET_HEADS * RET_DK, RET_HEADS * RET_DK, RET_HEADS * RET_DV, RET_HEADS * RET_DV,
              DIL_HEADS * DIL_DH, DIL_HEADS * DIL_DH, DIL_HEADS * DIL_DH)
EVEN_IN_2 = sum(EVEN_SIZES_2)
EVEN_MIX_2 = RET_HEADS * RET_DV + DIL_HEADS * DIL_DH
GLA_SIZES = (GLA_HEADS * GLA_DK, GLA_HEADS * GLA_DK, GLA_HEADS * GLA_DV, GLA_HEADS * GLA_DV, GLA_LOWRANK)
GLA_IN = sum(GLA_SIZES)
GLA_MIX = GLA_HEADS * GLA_DV


def _split(p, sizes):
    out, start = [], 0
    for s in sizes:
        out.append(p[..., start:start + s])
        start += s
    return out

def _rmsnorm(x, g):
    xf = x.astype(jnp.float32)
    y = xf * lax.rsqrt(jnp.mean(xf * xf, axis=-1, keepdims=True) + EPS)
    return (y * g.astype(jnp.float32)).astype(x.dtype)

def _head_norm(o):
    mu = jnp.mean(o, axis=-1, keepdims=True)
    var = jnp.mean(jnp.square(o - mu), axis=-1, keepdims=True)
    return (o - mu) * lax.rsqrt(var + EPS)

def _swiglu(h, wg, wu, wd):
    return (jax.nn.silu(h @ wg) * (h @ wu)) @ wd

def _rotary(x, inv_freq):
    rot = 2 * inv_freq.shape[0]
    pos = jnp.arange(x.shape[1], dtype=jnp.float32)
    ang = pos[:, None] * inv_freq[None, :]
    cos = jnp.cos(ang)[None, :, None, :].astype(x.dtype)
    sin = jnp.sin(ang)[None, :, None, :].astype(x.dtype)
    x1 = x[..., :rot // 2]
    x2 = x[..., rot // 2:rot]
    return jnp.concatenate([x1 * cos - x2 * sin, x2 * cos + x1 * sin, x[..., rot:]], axis=-1)

def _retention(q, k, v):
    B, S, H, Dk = q.shape
    Dv = v.shape[-1]
    C = RET_CHUNK
    N = S // C
    log_g = jnp.log(1.0 - 2.0 ** (-5.0 - jnp.arange(H, dtype=jnp.float32)))
    to_chunks = lambda t: t.reshape(B, N, C, H, t.shape[-1]).transpose(0, 3, 1, 2, 4)
    qc, kc, vc = to_chunks(q), to_chunks(k), to_chunks(v)
    i = jnp.arange(C, dtype=jnp.float32)
    rel = i[:, None] - i[None, :]
    dmask = jnp.where(rel >= 0, jnp.exp(log_g[:, None, None] * jnp.maximum(rel, 0.0)), 0.0)
    scores = jnp.einsum('bhnid,bhnjd->bhnij', qc, kc) * dmask[None, :, None]
    inner = jnp.einsum('bhnij,bhnje->bhnie', scores, vc)
    k_dec = kc * jnp.exp(log_g[:, None] * (C - 1 - i))[None, :, None, :, None]
    kv = jnp.einsum('bhnjd,bhnje->nbhde', k_dec, vc)
    chunk_decay = jnp.exp(log_g * C)[None, :, None, None]

    def step(s, kv_n):
        return s * chunk_decay + kv_n, s

    _, s_prev = lax.scan(step, jnp.zeros((B, H, Dk, Dv), jnp.float32), kv)
    q_dec = qc * jnp.exp(log_g[:, None] * (i + 1.0))[None, :, None, :, None]
    cross = jnp.einsum('bhnid,nbhde->bhnie', q_dec, s_prev)
    o = inner + cross
    return o.transpose(0, 2, 3, 1, 4).reshape(B, S, H, Dv)

def _dilated_branch(q, k, v, window, dil):
    B, S, H, Dh = q.shape
    L = S // dil
    W = window // dil
    c = DIL_BLOCK
    nb = -(-L // c)
    Lp = nb * c

    def split(t):
        return t.reshape(B, L, dil, H, Dh).transpose(0, 2, 3, 1, 4).reshape(B * dil, H, L, Dh)

    qs = jnp.pad(split(q), ((0, 0), (0, 0), (0, Lp - L), (0, 0))).reshape(B * dil, H, nb, c, Dh)

    def kblocks(t):
        t = jnp.pad(split(t), ((0, 0), (0, 0), (c, Lp - L), (0, 0))).reshape(B * dil, H, nb + 1, c, Dh)
        return jnp.concatenate([t[:, :, :-1], t[:, :, 1:]], axis=3)

    kb, vb = kblocks(k), kblocks(v)
    s = jnp.einsum('zhnqd,zhnkd->zhnqk', qs, kb).astype(jnp.float32) * (Dh ** -0.5)
    qi = jnp.arange(c)[:, None]
    kj = jnp.arange(2 * c)[None, :]
    dist = qi + c - kj
    blk = jnp.arange(nb)[:, None, None]
    valid = (dist >= 0) & (dist <= W) & (blk * c + kj - c >= 0)
    s = jnp.where(valid, s, -jnp.inf)
    m = jnp.max(s, axis=-1, keepdims=True)
    p = jnp.exp(s - m)
    l = jnp.sum(p, axis=-1, keepdims=True)
    o = jnp.einsum('zhnqk,zhnkd->zhnqd', p, vb.astype(jnp.float32)) / l
    lse = (m + jnp.log(l))[..., 0]
    o = o.reshape(B, dil, H, Lp, Dh)[:, :, :, :L].transpose(0, 3, 1, 2, 4).reshape(B, S, H, Dh)
    lse = lse.reshape(B, dil, H, Lp)[..., :L].transpose(0, 3, 1, 2).reshape(B, S, H)
    return o, lse

def _dilated_attention(q, k, v):
    outs, lses = [], []
    for window, dil in DIL_PATTERNS:
        o, lse = _dilated_branch(q, k, v, window, dil)
        outs.append(o)
        lses.append(lse)
    w = jax.nn.softmax(jnp.stack(lses, axis=0), axis=0)
    return jnp.sum(w[..., None] * jnp.stack(outs, axis=0), axis=0)

def _retention_dilated_mixer(h, w_in, w_out):
    B, S, _ = h.shape
    rq, rk, rv, rg, dq, dk, dv = _split(h @ w_in, EVEN_SIZES_2)
    ret_freq = RET_THETA ** (-jnp.linspace(0.0, 1.0, RET_DK // 2, dtype=jnp.float32))
    rq = _rotary(rq.reshape(B, S, RET_HEADS, RET_DK), ret_freq).astype(jnp.float32)
    rk = _rotary(rk.reshape(B, S, RET_HEADS, RET_DK), ret_freq).astype(jnp.float32) * (RET_DK ** -0.5)
    rv = rv.reshape(B, S, RET_HEADS, RET_DV).astype(jnp.float32)
    o_r = _head_norm(_retention(rq, rk, rv)).reshape(B, S, RET_HEADS * RET_DV)
    o_r = o_r * jax.nn.silu(rg.astype(jnp.float32))
    rope_freq = ROPE_THETA ** (-jnp.arange(0, ROT_DIM, 2, dtype=jnp.float32) / ROT_DIM)
    dq = _rotary(dq.reshape(B, S, DIL_HEADS, DIL_DH), rope_freq)
    dk = _rotary(dk.reshape(B, S, DIL_HEADS, DIL_DH), rope_freq)
    dv = dv.reshape(B, S, DIL_HEADS, DIL_DH)
    o_d = _dilated_attention(dq, dk, dv).reshape(B, S, DIL_HEADS * DIL_DH)
    cat = jnp.concatenate([o_r.astype(h.dtype), o_d.astype(h.dtype)], axis=-1)
    return cat @ w_out

def _gla(q, k, v, log_a):
    B, S, H, Dk = q.shape
    Dv = v.shape[-1]
    C = GLA_CHUNK
    N = S // C
    to_chunks = lambda t: t.reshape(B, N, C, H, t.shape[-1]).transpose(0, 3, 1, 2, 4)
    qc, kc, vc, lac = to_chunks(q), to_chunks(k), to_chunks(v), to_chunks(log_a)
    b = jnp.cumsum(lac, axis=3)
    b_last = b[:, :, :, -1:]
    q_t = qc * jnp.exp(b)
    k_t = kc * jnp.exp(-b)
    causal = jnp.tril(jnp.ones((C, C), dtype=bool))
    scores = jnp.where(causal, jnp.einsum('bhnid,bhnjd->bhnij', q_t, k_t), 0.0)
    inner = jnp.einsum('bhnij,bhnje->bhnie', scores, vc)
    kv = jnp.einsum('bhnjd,bhnje->nbhde', kc * jnp.exp(b_last - b), vc)
    decay = jnp.exp(b_last[:, :, :, 0]).transpose(2, 0, 1, 3)

    def step(s, inp):
        kv_n, d_n = inp
        return s * d_n[..., None] + kv_n, s

    _, s_prev = lax.scan(step, jnp.zeros((B, H, Dk, Dv), jnp.float32), (kv, decay))
    cross = jnp.einsum('bhnid,nbhde->bhnie', q_t, s_prev)
    o = inner + cross
    return o.transpose(0, 2, 3, 1, 4).reshape(B, S, H, Dv)

def _gla_mixer(h, w_in, w_a2, b_a, w_out):
    B, S, _ = h.shape
    q, k, v, r, a_low = _split(h @ w_in, GLA_SIZES)
    log_a = jax.nn.log_sigmoid((a_low @ w_a2 + b_a).astype(jnp.float32)) / GLA_TAU
    q = q.reshape(B, S, GLA_HEADS, GLA_DK).astype(jnp.float32) * (GLA_DK ** -0.5)
    k = k.reshape(B, S, GLA_HEADS, GLA_DK).astype(jnp.float32)
    v = v.reshape(B, S, GLA_HEADS, GLA_DV).astype(jnp.float32)
    log_a = log_a.reshape(B, S, GLA_HEADS, GLA_DK)
    o = _head_norm(_gla(q, k, v, log_a)).reshape(B, S, GLA_MIX)
    o = o * jax.nn.silu(r.astype(jnp.float32))
    return o.astype(h.dtype) @ w_out

def second_inputs(seed: int = 0) -> dict:
    key = jax.random.key(seed)
    ks = jax.random.split(key, 24)
    n_even = (DEPTH + 1) // 2
    n_odd = DEPTH // 2
    f32 = jnp.float32

    def w(k, shape, fan_in):
        return jax.random.normal(k, shape, f32) * (fan_in ** -0.5)

    def gain(k, shape):
        return 1.0 + 0.05 * jax.random.normal(k, shape, f32)

    return {
        "x": jax.random.normal(ks[0], (BATCH, SEQ, D_MODEL), f32),
        "ffn_pre_norm": gain(ks[1], (DEPTH, D_MODEL)),
        "ffn_pre_w_gate": w(ks[2], (DEPTH, D_MODEL, FFN_HIDDEN), D_MODEL),
        "ffn_pre_w_up": w(ks[3], (DEPTH, D_MODEL, FFN_HIDDEN), D_MODEL),
        "ffn_pre_w_down": w(ks[4], (DEPTH, FFN_HIDDEN, D_MODEL), FFN_HIDDEN),
        "mix_norm": gain(ks[5], (DEPTH, D_MODEL)),
        "ab_w_in": w(ks[6], (n_even, D_MODEL, EVEN_IN_2), D_MODEL),
        "ab_w_out": w(ks[7], (n_even, EVEN_MIX_2, D_MODEL), EVEN_MIX_2),
        "gla_w_in": w(ks[8], (n_odd, D_MODEL, GLA_IN), D_MODEL),
        "gla_w_a2": w(ks[9], (n_odd, GLA_LOWRANK, GLA_HEADS * GLA_DK), GLA_LOWRANK),
        "gla_b_a": 0.1 * jax.random.normal(ks[10], (n_odd, GLA_HEADS * GLA_DK), f32),
        "gla_w_out": w(ks[11], (n_odd, GLA_MIX, D_MODEL), GLA_MIX),
        "ffn_post_norm": gain(ks[12], (DEPTH, D_MODEL)),
        "ffn_post_w_gate": w(ks[13], (DEPTH, D_MODEL, FFN_HIDDEN), D_MODEL),
        "ffn_post_w_up": w(ks[14], (DEPTH, D_MODEL, FFN_HIDDEN), D_MODEL),
        "ffn_post_w_down": w(ks[15], (DEPTH, FFN_HIDDEN, D_MODEL), FFN_HIDDEN),
        "final_norm": gain(ks[16], (D_MODEL,)),
    }

def second_block(x, ffn_pre_norm, ffn_pre_w_gate, ffn_pre_w_up, ffn_pre_w_down, mix_norm,
              ab_w_in, ab_w_out, gla_w_in, gla_w_a2, gla_b_a, gla_w_out,
              ffn_post_norm, ffn_post_w_gate, ffn_post_w_up, ffn_post_w_down, final_norm):
    for l in range(DEPTH):
        h = _rmsnorm(x, ffn_pre_norm[l])
        x = x + 0.5 * _swiglu(h, ffn_pre_w_gate[l], ffn_pre_w_up[l], ffn_pre_w_down[l])
        h = _rmsnorm(x, mix_norm[l])
        if l % 2 == 0:
            x = x + _retention_dilated_mixer(h, ab_w_in[l // 2], ab_w_out[l // 2])
        else:
            x = x + _gla_mixer(h, gla_w_in[l // 2], gla_w_a2[l // 2], gla_b_a[l // 2], gla_w_out[l // 2])
        h = _rmsnorm(x, ffn_post_norm[l])
        x = x + 0.5 * _swiglu(h, ffn_post_w_gate[l], ffn_post_w_up[l], ffn_post_w_down[l])
    return _rmsnorm(x, final_norm)


def setup_inputs(seed=0):
    out = dict(first_inputs(seed))
    for name, value in second_inputs(seed + 1).items():
        if name != "x":
            out[name + "_2"] = value
    return out


def reference(
    x, mem, positions, ln_gains, ffn1_w_in, ffn1_w_out, ffn2_w_in, ffn2_w_out, even_w_in,
    even_f_bias, even_qk_gains, even_lambda, even_subln_gain, even_w_out, odd_w_in, odd_conv_w,
    odd_qk_gains, odd_rel_bias, odd_w_out, x_w_q, x_w_kv, x_qk_gains, x_w_o, ffn_pre_norm_2,
    ffn_pre_w_gate_2, ffn_pre_w_up_2, ffn_pre_w_down_2, mix_norm_2, ab_w_in_2, ab_w_out_2,
    gla_w_in_2, gla_w_a2_2, gla_b_a_2, gla_w_out_2, ffn_post_norm_2, ffn_post_w_gate_2,
    ffn_post_w_up_2, ffn_post_w_down_2, final_norm_2,
):
    x = first_block(
        x, mem, positions, ln_gains, ffn1_w_in, ffn1_w_out, ffn2_w_in, ffn2_w_out, even_w_in,
        even_f_bias, even_qk_gains, even_lambda, even_subln_gain, even_w_out, odd_w_in,
        odd_conv_w, odd_qk_gains, odd_rel_bias, odd_w_out, x_w_q, x_w_kv, x_qk_gains, x_w_o,
    )
    return second_block(
        x, ffn_pre_norm_2, ffn_pre_w_gate_2, ffn_pre_w_up_2, ffn_pre_w_down_2, mix_norm_2,
        ab_w_in_2, ab_w_out_2, gla_w_in_2, gla_w_a2_2, gla_b_a_2, gla_w_out_2, ffn_post_norm_2,
        ffn_post_w_gate_2, ffn_post_w_up_2, ffn_post_w_down_2, final_norm_2,
    )


_drawn_inputs = setup_inputs


def setup_inputs(seed=0):
    import zlib

    import numpy as np

    out = dict(_drawn_inputs(seed))
    spreads = {}
    factors = {'odd_qk_gains': 8.0,
     'x_qk_gains': 4.244,
     'gla_b_a_2': 17.194,
     'ffn_post_norm_2': 2.785,
     'ffn_pre_norm_2': 3.062,
     'gla_w_a2_2': 2.703,
     'mix_norm_2': 2.764}
    for name, (base, spread) in spreads.items():
        noise = np.random.default_rng([zlib.crc32(name.encode()), seed]).standard_normal(out[name].shape)
        drawn = base * np.exp(spread * noise) if base else spread * noise
        out[name] = jnp.asarray(drawn.astype(out[name].dtype))
    for name, factor in factors.items():
        out[name] = (out[name] * factor).astype(out[name].dtype)
    return out
```

```python
from collections import namedtuple
from contextlib import ExitStack

import numpy as np

import concourse.bass as bass
from concourse import mybir

F32 = mybir.dt.float32
F32R = mybir.dt.float32r
I32 = mybir.dt.int32
ALU = mybir.AluOpType
ACT = mybir.ActivationFunctionType
AX = mybir.AxisListType

P = 128
T = 256
D = 1024
KB = D // P
FF = 2816
HB = FF // P
CW = 256
EPS = 1e-6
LAMBDA_INIT = 0.8 - 0.6 * float(np.exp(-0.0))
GATE, UP, OTHER = range(3)
RING = 4
BANKS = 4




class Stages:
    pass


class Progress:

    def __init__(self):
        self.split = self.evac = self.chain = 0


class Counts:

    def __init__(self):
        self.norm = 0
        self.gen = 0
        self.head = 0
        self.rot = 0
        self.att = 0
        self.pv = 0
        self.blk = 0
        self.conv = 0
        self.mean = 0
        self.meanb = 0


Unit = namedtuple("Unit", "raw half k0 nk first last out mode src need")
Linear = namedtuple("Linear", "u0 u1 o0 o1")


def gain_columns():
    at, n = {}, 0
    for name, width in ([(f"ln{l}{j}", 8) for l in range(2) for j in range(5)]
                        + [("pre0", 8), ("pre1", 8), ("mix0", 8), ("mix1", 8), ("post0", 8), ("post1", 8), ("final", 8)]
                        + [("even", 4), ("odd", 2), ("subln", 1), ("x0", 4), ("x1", 4), ("conv", 12),
                           ("ba", 4), ("fb", 1)]):
        at[name] = n
        n += width
    return at, n


def plan_stream(io):
    loads, units, outs, lin = [], [], [], {}

    def add(name, chunks, rows, mode, src, need, frees=lambda c: OTHER):
        u0, o0 = len(units), len(outs)
        for c, (w, col) in enumerate(chunks):
            pieces = [(k, min(8, rows - k)) for k in range(0, rows, 8)]
            for k0, nk in pieces:
                loads.append((w[k0 * P:(k0 + nk) * P, col:col + CW].rearrange("(k p) n -> p k n", p=P), nk))
                for half in range(2):
                    out = o0 + 2 * c + half
                    first, last = k0 == 0, k0 + nk == rows
                    if last:
                        outs.append((len(units), frees(c)))
                    units.append(Unit(len(loads) - 1, half, k0, nk, first, last, out, mode, src,
                                      need if src != "hid" else HB * need + k0 + nk))
        lin[name] = Linear(u0, len(units), o0, len(outs))

    def cols(w, c0, n):
        return [(w, c0 + c) for c in range(0, n, CW)]

    gen = 0
    for n in range(2):
        def ffn(f, wi, wo):
            gu = [x for c in range(0, FF, CW) for x in ((wi, c), (wi, FF + c))]
            add(f"up{f}", gu, KB, "F", "hn", gen, lambda c: UP if c % 2 else GATE)
            add(f"down{f}", cols(wo, 0, D), HB, "F", "hid", f)
        ffn(2 * n, io["ffn1_w_in"][n], io["ffn1_w_out"][n])
        gen += 1
        add(f"memk{n}", cols(io["x_w_kv"][n], 0, D), KB, "F", "mn", n)
        if n == 0:
            w = io["even_w_in"][0]
            for name, c0, mode in (("aq", 0, "F"), ("ak", 512, "F"), ("av", 1024, "T"),
                                   ("bq", 1544, "F"), ("bk", 2056, "F"), ("bv", 2568, "T")):
                add(name, cols(w, c0, 512), KB, mode, "hn", gen)
            wo = io["even_w_out"][0]
        else:
            w = io["odd_w_in"][0]
            for i, name in enumerate(("cb", "cc", "ch", "dq", "dk", "dv")):
                add(name, cols(w, 512 * i, 512), KB, "T" if name == "dv" else "F", "hn", gen)
            wo = io["odd_w_out"][0]
        gen += 1
        add(f"mixout{n}", cols(wo, 0, D), KB, "F", "hn", gen)
        gen += 1
        add(f"memv{n}", cols(io["x_w_kv"][n], D, D), KB, "T", "mn", n)
        add(f"xq{n}", cols(io["x_w_q"][n], 0, D), KB, "F", "hn", gen)
        gen += 1
        add(f"xo{n}", cols(io["x_w_o"][n], 0, D), KB, "F", "hn", gen)
        gen += 1
        ffn(2 * n + 1, io["ffn2_w_in"][n], io["ffn2_w_out"][n])
        gen += 1
    for n in range(2):
        def ffn2(f, wg, wu, wo):
            gu = [x for c in range(0, FF, CW) for x in ((wg, c), (wu, c))]
            add(f"up{f}", gu, KB, "F", "hn", gen, lambda c: UP if c % 2 else GATE)
            add(f"down{f}", cols(wo, 0, D), HB, "F", "hid", f)
        ffn2(4 + 2 * n, io["ffn_pre_w_gate_2"][n], io["ffn_pre_w_up_2"][n], io["ffn_pre_w_down_2"][n])
        gen += 1
        if n == 0:
            w = io["ab_w_in_2"][0]
            for i, name in enumerate(("rq", "rk", "rv", "rg", "eq", "ek", "ev")):
                add(name, cols(w, 512 * i, 512), KB, "T" if name in ("rv", "ev") else "F", "hn", gen)
            wo = io["ab_w_out_2"][0]
        else:
            w = io["gla_w_in_2"][0]
            for name, c0, width, mode in (("gq", 0, 512, "F"), ("gk", 512, 512, "F"), ("gv", 1024, 1024, "T"),
                                          ("gr", 2048, 1024, "F")):
                add(name, cols(w, c0, width), KB, mode, "hn", gen)
            wo = io["gla_w_out_2"][0]
        gen += 1
        add(f"mixout{2 + n}", cols(wo, 0, D), KB, "F", "hn", gen)
        gen += 1
        ffn2(5 + 2 * n, io["ffn_post_w_gate_2"][n], io["ffn_post_w_up_2"][n], io["ffn_post_w_down_2"][n])
        gen += 1
    return loads, units, outs, lin


def build(nc, io, out):
    loads, units, outs, lin = plan_stream(io)
    GC, NG = gain_columns()
    freed, count = [], [0, 0, 0]
    for _, kind in outs:
        count[kind] += 1
        freed.append((kind, count[kind]))
    last_of_load = {u.raw: i for i, u in enumerate(units)}
    last_reader = {}
    for i, u in enumerate(units):
        if u.src != "hid":
            last_reader[u.src, u.need] = i
    last_hid_reader = [lin[f"down{f}"].u1 - 1 for f in range(8)]

    with ExitStack() as ctx:
        def sb(name, shape, dt=F32):
            return ctx.enter_context(nc.sbuf_tensor(name, shape, dt))

        def sem(name):
            return ctx.enter_context(nc.semaphore(name))

        x = sb("x", [P, KB, T])
        hn_hi = sb("hn_hi", [P, KB, T], F32R)
        hn_lo = sb("hn_lo", [P, KB, T], F32R)
        mn_hi = sb("mn_hi", [P, KB, T], F32R)
        mn_lo = sb("mn_lo", [P, KB, T], F32R)
        raw = sb("raw", [P, RING, 8, CW])
        w_hi = sb("w_hi", [P, RING, 8, P], F32R)
        w_lo = sb("w_lo", [P, RING, 8, P], F32R)
        t1 = sb("t1", [P, KB, T])
        t2 = sb("t2", [P, KB, T])
        keep = sb("keep", [P, 16, T])
        prob = sb("prob", [P, 3, 2, T])
        probT = sb("probT", [P, 2, 2, T])
        gains = sb("gains", [P, NG])
        mats = sb("mats", [P, 7, P])
        colc = sb("colc", [P, 4])
        silu_g = sb("silu_g", [P, 2, T])
        hidf = sb("hidf", [P, 2, T])
        small = sb("small", [P, 64])
        small_w = sb("small_w", [P, KB, 16])
        wa2 = sb("wa2", [16, 512])
        pos = sb("pos", [P, T], I32)
        with nc.sbuf_tensor("hid_hi", [P, HB, T], F32R) as hid_hi, nc.sbuf_tensor("hid_lo", [P, HB, T], F32R) as hid_lo:
            pass
        work = sb("work", [P, 2 * HB, T])
        ident, ones, ones64, perm_rope, perm_ret = (mats[:, i, :] for i in range(5))
        reverse = mats[:, 6, :]
        key_before = mats[:, 5, 0:64]
        eps_col, rope_freq = colc[:, 0:1], colc[:, 1:2]

        acc = ctx.enter_context(nc.psum_tensor("acc", [P, BANKS, 512], F32))
        wide = ctx.enter_context(nc.psum_tensor("wide", [P, 4, 512], F32))

        raw_in = [sem(f"raw_in{i}") for i in range(RING)]
        w_hi_ready, w_lo_ready, unit_done = sem("w_hi_ready"), sem("w_lo_ready"), sem("unit_done")
        gate_evac, out_evac = sem("gate_evac"), sem("out_evac")
        hn_hi_ready, hn_lo_ready = sem("hn_hi_ready"), sem("hn_lo_ready")
        mn_hi_ready, mn_lo_ready = sem("mn_hi_ready"), sem("mn_lo_ready")
        hid_mul, hid_hi_ready, hid_lo_ready = sem("hid_mul"), sem("hid_hi_ready"), sem("hid_lo_ready")
        squares, sums_done, std_done, normed = sem("squares"), sem("sums_done"), sem("std_done"), sem("normed")
        const_in, mem_in, x_in = sem("const_in"), sem("mem_in"), sem("x_in")
        dve_chain, act_chain, pool_chain = sem("dve_chain"), sem("act_chain"), sem("pool_chain")
        head_sq, head_sums, head_std, head_normed = sem("head_sq"), sem("head_sums"), sem("head_std"), sem("head_normed")
        rot_done, rot_added = sem("rot_done"), sem("rot_added")
        scores, biased, expd, probs, turned, turned_copied = (
            sem("scores"), sem("biased"), sem("expd"), sem("probs"), sem("turned"), sem("turned_copied"))
        attended, att_out = sem("attended"), sem("att_out")
        masks_in, pos_in, lam_in, wf_in, wa_in, tables_in = (
            sem("masks_in"), sem("pos_in"), sem("lam_in"), sem("wf_in"), sem("wa_in"), sem("tables_in"))
        gate_mm, gate_step = sem("gate_mm"), sem("gate_step")
        rope_step = sem("rope_step")
        lam_step = sem("lam_step")
        conv_done = sem("conv_done")
        ret_s, ret_p, ret_o, ret_copied = sem("ret_s"), sem("ret_p"), sem("ret_o"), sem("ret_copied")
        gla_mm, gla_dve, gla_act = sem("gla_mm"), sem("gla_dve"), sem("gla_act")
        mean_off, mean_sums, mean_act, mean_normed = sem("mean_off"), sem("mean_sums"), sem("mean_act"), sem("mean_normed")
        final_out = sem("final_out")
        band_in, band_turned, band_masked = sem("band_in"), sem("band_turned"), sem("band_masked")

        memk = work[:, 0:8, :]
        memv = work[:, 8:16, :].rearrange("p b t -> p (b t)").rearrange("p (i n) -> p i n", i=2)
        cat = keep[:, 0:8, :]

        def vals(a, nb):
            return work[:, a:a + nb, :].rearrange("p b t -> p (b t)").rearrange("p (i n) -> p i n", i=2)

        dest = {"aq": 16, "ak": 20, "bq": 24, "bk": 28, "av": 32, "bv": 36,
                "dq": 16, "dk": 20, "cb": 24, "cc": 28, "ch": 32, "dv": 36,
                "rq": 16, "rk": 20, "rg": 24, "eq": 28, "ek": 32, "rv": 36, "ev": 40,
                "gq": 16, "gk": 20, "gr": 24, "gv": 32,
                "memk0": 0, "memk1": 0, "memv0": 8, "memv1": 8, "xq0": 16, "xq1": 16}
        nblk = {n: (lin[n].o1 - lin[n].o0) for n in dest}

        causal, chunked = keep[:, 8:10, :], keep[:, 10:12, :]
        rope_c, rope_s = keep[:, 12:13, :], keep[:, 13:14, :]
        dil_bias = work[:, 4:6, :]
        chunked_odd = work[:, 40:42, :]
        ret_c, ret_sn = work[:, 0:1, :], work[:, 1:2, :]
        dil_c, dil_sn = work[:, 2:3, :], work[:, 3:4, :]
        decay = keep[:, 8:16, :].rearrange("p (h k) t -> p h k t", h=4)

        def band(h):
            return work[:, 8 + 2 * h:10 + 2 * h, :] if h < 4 else keep[:, 8 + 2 * (h - 4):10 + 2 * (h - 4), :]

        cum, ncum = keep[0:8, 14, :], keep[0:8, 15, :]

        def half(a, h):
            return work[64 * (h % 2):64 * (h % 2) + 64, a + h // 2, :]

        def attention(kind):
            if kind == "A":
                v = vals(32, 4)
                return ([([half(16, h)], [half(20, h)], causal, h, None) for h in range(8)],
                        [(h, [(v[:, :, 64 * h:64 * h + 64], h // 2, 64 * (h % 2))]) for h in range(8)], 0.125)
            if kind == "B":
                v = vals(36, 4)
                return ([([half(24, i)], [half(28, i)], chunked, None, i - 1 if i % 2 else None) for i in range(8)],
                        [(2 * h + 1, [(v[:, :, P * h:P * h + P], 4 + h, 0)]) for h in range(4)], 0.125)
            if kind == "D":
                v = vals(36, 4)
                return ([([half(16, h)], [half(20, h)], band(h), None, None) for h in range(8)],
                        [(h, [(v[:, :, 64 * h:64 * h + 64], 4 + h // 2, 64 * (h % 2))]) for h in range(8)], 0.125)
            if kind == "E":
                v = vals(40, 4)
                return ([([half(28, h)], [half(32, h)], dil_bias, None, None) for h in range(8)],
                        [(h, [(v[:, :, 64 * h:64 * h + 64], 4 + h // 2, 64 * (h % 2))]) for h in range(8)], 0.125)
            return ([([work[:, 16 + 2 * h, :], work[:, 17 + 2 * h, :]], [work[:, 2 * h, :], work[:, 2 * h + 1, :]],
                      None, None, None) for h in range(4)],
                    [(h, [(memv[:, :, CW * h + P * e:CW * h + P * e + P], 2 * h + e, 0) for e in range(2)])
                     for h in range(4)], 0.0625)

        def order(s):
            c = Counts()

            def finish(gain, last=False):
                s.norm_finish(c.norm, GC[gain], c.gen, last)
                c.norm += 1
                c.gen += 1

            def head(src, nb, per, gain):
                s.head_norm(c, src, nb, per, gain)
                c.head += 1

            def att(kind):
                items, pvs, scale = attention(kind)
                s.attend(c, items, pvs, scale)
                c.att += len(items)
                c.pv += len(pvs)
                c.blk += len({b for _, l in pvs for _, b, _ in l})

            def mean(nb, per, gate):
                s.mean_norm(c, nb, per, gate)
                c.mean += 1
                c.meanb += nb

            def split_cat():
                s.cat_split(c)
                c.gen += 1

            s.setup()
            s.first_squares(c.norm)
            for n in range(2):
                finish(f"ln{n}0")
                s.ffn_up(2 * n, n, c.norm, GC[f"ln{n}3"], c.gen)
                c.norm += 1
                s.residual(f"down{2 * n}", 0.5, c.norm)
                finish(f"ln{n}1")
                s.project(f"memk{n}")
                if n == 0:
                    s.forget_gates(c.norm)
                    for name in ("aq", "ak", "av", "bq", "bk", "bv"):
                        s.project(name)
                    head(work[:, 16:24, :], 8, 64, ["even"] * 4 + [("even", 1)] * 4)
                    att("A")
                    head(work[:, 24:32, :], 8, 64, [("even", 2)] * 4 + [("even", 3)] * 4)
                    s.rotate(c, work[:, 24:32, :], perm_rope, rope_c, rope_s)
                    c.rot += 4
                    att("B")
                    head(cat[:, 4:8, :], 4, 128, ["subln"] * 4)
                else:
                    for name in ("cb", "cc", "ch", "dq", "dk", "dv"):
                        s.project(name)
                    s.band_bias()
                    s.conv()
                    c.conv += 1
                    head(work[:, 16:24, :], 8, 64, ["odd"] * 4 + [("odd", 1)] * 4)
                    att("D")
                split_cat()
                s.residual(f"mixout{n}", 1.0, c.norm)
                s.project(f"memv{n}")
                finish(f"ln{n}2")
                s.project(f"xq{n}")
                head(memk, 8, 256, [(f"x{n}", 2 + b % 2) for b in range(8)])
                head(work[:, 16:24, :], 8, 256, [(f"x{n}", b % 2) for b in range(8)])
                att("X")
                split_cat()
                s.residual(f"xo{n}", 1.0, c.norm)
                finish(f"ln{n}4")
                s.ffn_up(2 * n + 1, None, None, None, c.gen)
                s.residual(f"down{2 * n + 1}", 0.5, c.norm)
            for n in range(2):
                finish(f"pre{n}")
                s.ffn_up(4 + 2 * n, None, None, None, c.gen)
                s.residual(f"down{4 + 2 * n}", 0.5, c.norm)
                finish(f"mix{n}")
                if n == 0:
                    s.tables_2()
                    for name in ("rq", "rk", "rv", "rg", "eq", "ek", "ev"):
                        s.project(name)
                    s.rotate(c, work[:, 16:24, :], perm_ret, ret_c, ret_sn)
                    c.rot += 4
                    s.retention()
                    mean(4, 1, work[:, 24:28, :])
                    s.rotate(c, work[:, 28:36, :], perm_rope, dil_c, dil_sn)
                    c.rot += 4
                    att("E")
                else:
                    s.gla_gates(c.norm)
                    for name in ("gq", "gk", "gv", "gr"):
                        s.project(name)
                    s.gla()
                    mean(8, 2, work[:, 24:32, :])
                split_cat()
                s.residual(f"mixout{2 + n}", 1.0, c.norm)
                finish(f"post{n}")
                s.ffn_up(5 + 2 * n, None, None, None, c.gen)
                s.residual(f"down{5 + 2 * n}", 0.5, c.norm)
            finish("final", True)

        def gain_col(g, dim=None):
            name, i = g if isinstance(g, tuple) else (g, 0)
            return gains[:, GC[name] + i:GC[name] + i + 1]

        def out_ap(o, mode):
            a = acc[:, o % BANKS, 0:T]
            return a if mode == "F" else a.rearrange("p (i n) -> p i n", i=2)

        def wait_free(eng, o):
            if o >= BANKS:
                kind, n = freed[o - BANKS]
                eng.wait_ge((gate_evac, hid_mul, out_evac)[kind], n)

        def dest_ap(name, i):
            a = dest[name]
            if units[lin[name].u0].mode == "F":
                return work[:, a + i, :]
            return vals(a, nblk[name])[:, :, P * i:P * i + P]

        norms_total = 17
        g_q, g_k, g_v = work[:, 16:20, :], work[:, 20:24, :], vals(32, 8)
        g_kdec, g_kdecT = t1[:, 0:4, :], t1[:, 4:8, :]
        g_scores = prob[:, 0:2, :, :].rearrange("p s a t -> p (s a t)").rearrange("p (h n q) -> p h n q", h=4, n=4)
        g_state = work[:, 4:16, :].rearrange("p (n h) e -> p n h e", n=3)
        g_decay = small[:, 0:16]
        nmax = small[:, 16:22].rearrange("p (s q) -> p s q", s=3)
        rsum = small[:, 22:28].rearrange("p (s q) -> p s q", s=3)
        rinv = small[:, 28:34].rearrange("p (s q) -> p s q", s=3)
        rinv_lam = small[:, 34:36]
        lam_sum, lam_exp, neg_lam = small[:, 40:42], small[:, 42:44], small[:, 44:45]

        fills = {"hn": (hn_hi, hn_lo, hn_hi_ready, hn_lo_ready), "mn": (mn_hi, mn_lo, mn_hi_ready, mn_lo_ready)}

        def forget_z(i):
            return t2[0:8, 2 + i, :]

        block = ctx.enter_context(nc.Block())

        @block.sync
        def _(sp):
            sp.dma_start(x[:, :, :], io["x"].rearrange("(k p) t -> p k t", p=P)).then_inc(x_in, 16)
            sp.dma_start(gains[:, :], io["gains"]).then_inc(const_in, 16)
            sp.dma_start(mats[:, :, :], io["mats"]).then_inc(const_in, 16)
            sp.dma_start(colc[:, :], io["cols"]).then_inc(const_in, 16)
            for r, (src, nk) in enumerate(loads):
                if r >= RING:
                    sp.wait_ge(w_lo_ready, last_of_load[r - RING] + 1)
                sp.dma_start(raw[:, r % RING, 0:nk, :], src).then_inc(raw_in[r % RING], 16)
            sp.wait_ge(normed, 8 * norms_total)
            sp.dma_start(out.rearrange("(k p) t -> p k t", p=P), t1[:, :, :]).then_inc(final_out, 16)
            sp.wait_ge(final_out, 16)

        @block.tensor
        def _(pe):
            s = Stages()

            def unit(i):
                u = units[i]
                if u.first:
                    wait_free(pe, u.out)
                pe.wait_ge(w_hi_ready, i + 1)
                if u.src == "hid":
                    a_hi, a_lo = hid_hi, hid_lo
                    pe.wait_ge(hid_hi_ready, u.need)
                    pe.wait_ge(hid_lo_ready, u.need)
                else:
                    a_hi, a_lo, r_hi, r_lo = fills[u.src]
                fresh = u.src != "hid" and (i == 0 or (units[i - 1].src, units[i - 1].need) != (u.src, u.need))
                wh, wl = w_hi[:, i % RING], w_lo[:, i % RING]
                bank = acc[:, u.out % BANKS, 0:T]
                if u.mode == "F":
                    for j in range(u.nk):
                        if fresh:
                            pe.wait_ge(r_hi, 8 * u.need + j + 1)
                            pe.wait_ge(r_lo, 8 * u.need + j + 1)
                        nc.tensor.matmul(bank, wh[:, j, :], a_hi[:, u.k0 + j, :], start=u.first and j == 0, stop=False)
                        nc.tensor.matmul(bank, wh[:, j, :], a_lo[:, u.k0 + j, :], start=False, stop=False)
                    pe.wait_ge(w_lo_ready, i + 1)
                    for j in range(u.nk):
                        mm = nc.tensor.matmul(bank, wl[:, j, :], a_hi[:, u.k0 + j, :], start=False,
                                              stop=u.last and j == u.nk - 1)
                else:
                    if fresh:
                        pe.wait_ge(r_hi, 8 * u.need + 8)
                        pe.wait_ge(r_lo, 8 * u.need + 8)
                    pe.wait_ge(w_lo_ready, i + 1)
                    for t in range(2):
                        half_bank = bank[:, P * t:P * t + P]
                        for j in range(u.nk):
                            ah, al = a_hi[:, j, P * t:P * t + P], a_lo[:, j, P * t:P * t + P]
                            nc.tensor.matmul(half_bank, ah, wh[:, j, :], start=j == 0, stop=False)
                            nc.tensor.matmul(half_bank, ah, wl[:, j, :], start=False, stop=False)
                            mm = nc.tensor.matmul(half_bank, al, wh[:, j, :], start=False, stop=j == u.nk - 1)
                mm.then_inc(unit_done, 1)

            def project(name):
                for i in range(lin[name].u0, lin[name].u1):
                    unit(i)

            def sum_squares(i, bank, k):
                pe.wait_ge(squares, 8 * i + k + 1)
                mm = nc.tensor.matmul(wide[:, bank, 0:T], ones, t1[:, k, :], start=k == 0, stop=k == 7)
                if k == 7:
                    mm.then_inc(sums_done, 1)

            def setup():
                pe.wait_ge(const_in, 48)

            def first_squares(i):
                for k in range(8):
                    sum_squares(i, 0, k)

            def residual(name, scale, i):
                l, ready = lin[name], []
                for n in range(l.u0, l.u1):
                    unit(n)
                    if units[n].last:
                        ready.append(units[n].out - l.o0)
                    while len(ready) > 2 and not units[n].last or len(ready) > 2:
                        sum_squares(i, 0, ready.pop(0))
                for k in ready:
                    sum_squares(i, 0, k)

            def ffn_up(f, n, mi, gain, gen):
                l = lin[f"up{f}"]
                for j, i in enumerate(range(l.u0, l.u1)):
                    unit(i)
                    if n is not None and j == 11:
                        for k in range(8):
                            sum_squares(mi, 1, k)

            def head_norm(c, src, nb, per, gain):
                pe.wait_ge(head_sq, c.head + 1)
                if per == 256:
                    for h in range(nb // 2):
                        for e in range(2):
                            mm = nc.tensor.matmul(wide[:, h, 0:T], ones, t1[:, 2 * h + e, :], start=e == 0, stop=e == 1)
                else:
                    m = ones64 if per == 64 else ones
                    for b in range(nb // 2):
                        mm = nc.tensor.matmul(wide[:, b, :], m, t1[:, 2 * b:2 * b + 2, :].rearrange("p b t -> p (b t)"),
                                              start=True, stop=True)
                mm.then_inc(head_sums, 1)

            def rotate(c, src, perm, cs, sn):
                if c.rot == 0:
                    pe.wait_ge(head_normed, c.head)
                elif c.rot == 4:
                    pe.wait_ge(out_evac, freed[lin["ev"].o1 - 1][1])
                else:
                    pe.wait_ge(mean_act, 3)
                for b in range(4):
                    pe_rot = nc.tensor.matmul(wide[:, b, :], perm, src[:, 2 * b:2 * b + 2, :].rearrange("p b t -> p (b t)"),
                                              start=True, stop=True)
                    pe_rot.then_inc(rot_done, 1)

            def attend(c, items, pvs, scale):
                pv_of = {it: n for n, (it, _) in enumerate(pvs)}
                blocks = sorted({b for _, l in pvs for _, b, _ in l})
                pe.wait_ge(head_normed, c.head)
                if c.rot:
                    pe.wait_ge(rot_added, c.rot)
                if items[0][3] is not None:
                    pe.wait_ge(gate_step, 4)
                for i in range(len(items) + 3):
                    if i < len(items):
                        q, k, bias, gate, _ = items[i]
                        if i >= 2:
                            pe.wait_ge(biased, c.att + i - 1)
                        for t in range(2):
                            o = wide[:, i % 2, T * t:T * t + T]
                            for e in range(len(q)):
                                mm = nc.tensor.matmul(o, q[e][:, P * t:P * t + P], k[e],
                                                      start=e == 0, stop=e == len(q) - 1 and gate is None)
                            if gate is not None:
                                row = ident[0:8, gate:gate + 1]
                                nc.tensor.matmul(o, cum[:, P * t:P * t + P], row.to_broadcast([8, T]), start=False, stop=False)
                                mm = nc.tensor.matmul(o, row.to_broadcast([8, P]), ncum, start=False, stop=True)
                        mm.then_inc(scores, 1)
                    if i - 2 in pv_of:
                        n = pv_of[i - 2]
                        pe.wait_ge(probs, c.att + i - 1)
                        if n >= 2:
                            pe.wait_ge(turned_copied, c.pv + n - 1)
                        p = prob[:, (c.att + i - 2) % 3]
                        for kt in range(2):
                            for qt in range(2):
                                mm = nc.tensor.transpose(wide[:, 2 + n % 2, T * kt + P * qt:T * kt + P * qt + P],
                                                         p[:, qt, P * kt:P * kt + P], ident)
                        mm.then_inc(turned, 1)
                    if i - 3 in pv_of:
                        n = pv_of[i - 3]
                        pe.wait_ge(turned_copied, c.pv + n + 1)
                        for v, b, p0 in pvs[n][1]:
                            at = blocks.index(b)
                            if at >= 4 and p0 == 0:
                                pe.wait_ge(att_out, c.blk + at - 3)
                            m = v.shape[2]
                            for kt in range(2):
                                mm = nc.tensor.matmul(acc[p0:p0 + m, at % 4, 0:T], v[:, kt, :], probT[:, n % 2, kt, :],
                                                      start=kt == 0, stop=kt == 1)
                        mm.then_inc(attended, 1)

            def band_bias():
                pe.wait_ge(band_in, 16 * 9)
                for h in range(8):
                    if h >= 4:
                        pe.wait_ge(band_masked, h - 3)
                    nc.tensor.matmul(wide[:, h % 4, :], reverse, band(h).rearrange("p q k -> p (q k)"), start=True, stop=True)\
                        .then_inc(band_turned, 1)

            def forget_gates(norms):
                pe.wait_ge(wf_in, 16)
                pe.wait_ge(normed, 8 * norms)
                for k in range(8):
                    mm = nc.tensor.matmul(wide[0:8, 1, 0:T], small_w[:, k, 0:8], t1[:, k, :], start=k == 0, stop=k == 7)
                mm.then_inc(gate_mm, 1)

            def retention():
                pe.wait_ge(rot_added, 8)
                v = vals(36, 4)
                for h in range(4):
                    if h >= 2:
                        pe.wait_ge(ret_p, h - 1)
                    for kt in range(2):
                        mm = nc.tensor.matmul(wide[:, h % 2, T * kt:T * kt + T], work[:, 20 + h, P * kt:P * kt + P],
                                              work[:, 16 + h, :], start=True, stop=True)
                    mm.then_inc(ret_s, 1)
                    if h >= 1:
                        ret_out(h - 1, v)
                ret_out(3, v)

            def ret_out(h, v):
                pe.wait_ge(ret_p, h + 1)
                for kt in range(2):
                    mm = nc.tensor.matmul(acc[:, h, 0:T], v[:, kt, P * h:P * h + P], probT[:, h % 2, kt, :],
                                          start=kt == 0, stop=kt == 1)
                mm.then_inc(ret_o, 1)

            def mean_norm(c, nb, per, gate):
                for step in range(2):
                    if step:
                        pe.wait_ge(mean_act, 3 * c.mean + 1)
                    elif c.mean == 0:
                        pe.wait_ge(ret_copied, 4)
                    else:
                        pe.wait_ge(gla_dve, 26)
                    src = cat if step == 0 else t1
                    for h in range(nb // per):
                        for e in range(per):
                            mm = nc.tensor.matmul(wide[:, h, 0:T], ones, src[:, per * h + e, :], start=e == 0, stop=e == per - 1)
                    mm.then_inc(mean_sums, 1)

            def gla_gates(norms):
                pe.wait_ge(wa_in, 32)
                pe.wait_ge(normed, 8 * norms)
                for k in range(8):
                    mm = nc.tensor.matmul(wide[0:16, 1, 0:T], small_w[:, k, :], t1[:, k, :], start=k == 0, stop=k == 7)
                mm.then_inc(gla_mm, 1)
                pe.wait_ge(gla_dve, 1)
                for h in range(4):
                    mm = nc.tensor.matmul(wide[:, h, 0:T], wa2[0:16, P * h:P * h + P], t2[0:16, 6, :], start=True, stop=True)
                mm.then_inc(gla_mm, 1)

            def gla():
                pe.wait_ge(gla_dve, 5)
                pe.wait_ge(out_evac, freed[lin["gr"].o1 - 1][1])
                for h in range(4):
                    for t in range(2):
                        mm = nc.tensor.transpose(wide[:, h // 2, T * (h % 2) + P * t:T * (h % 2) + P * t + P],
                                                 g_kdec[:, h, P * t:P * t + P], ident)
                mm.then_inc(gla_mm, 1)
                for h in range(4):
                    for n in range(4):
                        mm = nc.tensor.matmul(wide[64 * (n % 2):64 * (n % 2) + 64, 2, P * h + 64 * (n // 2):P * h + 64 * (n // 2) + 64],
                                              g_k[:, h, 64 * n:64 * n + 64], g_q[:, h, 64 * n:64 * n + 64], start=True, stop=True)
                mm.then_inc(gla_mm, 1)
                pe.wait_ge(gla_act, 7)
                for n in range(3):
                    for h in range(4):
                        if n:
                            pe.wait_ge(gla_dve, 6 + 4 * (n - 1) + h + 1)
                        p0 = 64 * (n % 2)
                        mm = nc.tensor.matmul(acc[:, h, 0:T], g_kdecT[p0:p0 + 64, h, P * (n // 2):P * (n // 2) + P],
                                              g_v[p0:p0 + 64, n // 2, CW * h:CW * h + CW], start=True, stop=True)
                        mm.then_inc(gla_mm, 1)
                pe.wait_ge(gla_dve, 18)
                for b in range(8):
                    h, e = b // 2, b % 2
                    if b >= 4:
                        pe.wait_ge(gla_dve, 18 + b - 3)
                    for n in range(4):
                        o = acc[:, b % 4, 64 * n:64 * n + 64]
                        mm = nc.tensor.matmul(o, g_v[:, n // 2, CW * h + P * e:CW * h + P * e + P],
                                              g_scores[:, h, n, :], start=True, stop=n == 0)
                        if n:
                            mm = nc.tensor.matmul(o, g_state[:, n - 1, h, P * e:P * e + P], g_q[:, h, 64 * n:64 * n + 64],
                                                  start=False, stop=True)
                    mm.then_inc(gla_mm, 1)

            s.setup, s.first_squares, s.residual, s.ffn_up, s.project = setup, first_squares, residual, ffn_up, project
            s.band_bias = band_bias
            s.norm_finish = s.cat_split = s.conv = s.tables_2 = lambda *a: None
            s.head_norm, s.rotate, s.attend, s.forget_gates = head_norm, rotate, attend, forget_gates
            s.retention, s.mean_norm, s.gla_gates, s.gla = retention, mean_norm, gla_gates, gla
            order(s)

        @block.scalar
        def _(act):
            s = Stages()
            state = Progress()

            def split_to(n):
                while state.split < min(n, len(units)):
                    i = state.split
                    u = units[i]
                    act.wait_ge(raw_in[u.raw % RING], 16 * (u.raw // RING + 1))
                    if i >= RING:
                        act.wait_ge(unit_done, i - RING + 1)
                    nc.scalar.activation(w_hi[:, i % RING, 0:u.nk, :], raw[:, u.raw % RING, 0:u.nk, P * u.half:P * u.half + P],
                                         ACT.Copy).then_inc(w_hi_ready, 1)
                    state.split += 1

            def setup():
                act.wait_ge(x_in, 16)
                act.wait_ge(const_in, 48)

            def first_squares(i):
                for k in range(8):
                    nc.scalar.activation(t1[:, k, :], x[:, k, :], ACT.Square).then_inc(squares, 1)
                split_to(RING)
                act.wait_ge(lam_step, 1)
                nc.scalar.activation(lam_exp, lam_sum, ACT.Exp).then_inc(lam_step, 1)
                act.wait_ge(rope_step, 1)
                nc.scalar.activation(rope_s, hidf[:, 0:1, :], ACT.Sin).then_inc(rope_step, 1)
                nc.scalar.activation(hidf[:, 1:2, :], hidf[:, 0:1, :], ACT.Sin, scale=0.5).then_inc(rope_step, 1)

            def finish(i, bank, kind, need, last=False):
                act.wait_ge(sums_done, i + 1)
                nc.scalar.activation(t2[:, 0, :], wide[:, bank, 0:T], ACT.Sqrt, scale=1.0 / D, bias=eps_col).then_inc(std_done, 1)
                if last:
                    return
                hi, lo, hi_ready, lo_ready = fills[kind]
                if need:
                    act.wait_ge(unit_done, last_reader[kind, need - 1] + 1)
                for k in range(8):
                    act.wait_ge(normed, 8 * i + k + 1)
                    nc.scalar.activation(hi[:, k, :], t1[:, k, :], ACT.Copy).then_inc(hi_ready, 1)

            def norm_finish(i, gain, gen, last):
                finish(i, 0, "hn", gen, last)

            def cat_split(c):
                act.wait_ge(att_out, c.blk) if c.blk else None
                act.wait_ge(head_normed, c.head)
                if c.conv:
                    act.wait_ge(conv_done, c.conv)
                if c.mean:
                    act.wait_ge(mean_normed, c.meanb)
                act.wait_ge(unit_done, last_reader["hn", c.gen - 1] + 1)
                for k in range(8):
                    nc.scalar.activation(hn_hi[:, k, :], cat[:, k, :], ACT.Copy).then_inc(hn_hi_ready, 1)

            def project(name):
                for i in range(lin[name].u0, lin[name].u1):
                    split_to(i + RING + 1)
                state.evac = freed[lin[name].o1 - 1][1]

            def residual(name, scale, i):
                l = lin[name]
                for n in range(l.u0, l.u1):
                    u = units[n]
                    if u.last:
                        act.wait_ge(out_evac, freed[u.out][1])
                        nc.scalar.activation(t1[:, u.out - l.o0, :], x[:, u.out - l.o0, :], ACT.Square).then_inc(squares, 1)
                    split_to(n + RING + 1)

            def ffn_up(f, n, mi, gain, gen):
                l = lin[f"up{f}"]
                if f:
                    act.wait_ge(unit_done, last_hid_reader[f - 1] + 1)
                for ch in range(FF // CW):
                    u0, m0 = l.u0 + 4 * ch, HB * f + 2 * ch
                    for h in range(2):
                        act.wait_ge(unit_done, u0 + h + 1)
                        if m0:
                            act.wait_ge(hid_mul, m0 - 1 + h)
                        nc.scalar.activation(silu_g[:, h, :], acc[:, units[u0 + h].out % BANKS, 0:T], ACT.Silu)\
                            .then_inc(gate_evac, 1)
                        split_to(u0 + h + RING + 1)
                    for h in range(2):
                        split_to(u0 + 2 + h + RING + 1)
                        act.wait_ge(hid_mul, m0 + h + 1)
                        nc.scalar.activation(hid_hi[:, 2 * ch + h, :], hidf[:, h, :], ACT.Copy).then_inc(hid_hi_ready, 1)
                    if n is not None and ch == 1:
                        act.wait_ge(mem_in, 16 * (n + 1))
                        act.wait_ge(hn_lo_ready, 8 * gen)
                        for k in range(8):
                            nc.scalar.activation(t1[:, k, :], keep[:, k, :], ACT.Square).then_inc(squares, 1)
                    if n is not None and ch == 3:
                        finish(mi, 1, "mn", n)

            def head_norm(c, src, nb, per, gain):
                act.wait_ge(out_evac, state.evac)
                act.wait_ge(hn_lo_ready, 8 * c.gen)
                act.wait_ge(gate_mm, 1)
                if c.blk:
                    act.wait_ge(att_out, c.blk)
                if c.conv:
                    act.wait_ge(conv_done, c.conv)
                if c.head:
                    act.wait_ge(head_normed, c.head)
                nc.scalar.activation(t1[:, 0:nb, :], src, ACT.Square).then_inc(head_sq, 1)
                act.wait_ge(head_sums, c.head + 1)
                if per == 256:
                    o, i = t2[:, 0:nb // 2, :], wide[:, 0:nb // 2, 0:T]
                else:
                    o, i = t2[:, 0:nb, :].rearrange("p (b a) t -> p b (a t)", a=2), wide[:, 0:nb // 2, :]
                nc.scalar.activation(o, i, ACT.Sqrt, scale=1.0 / per, bias=eps_col).then_inc(head_std, 1)

            def attend(c, items, pvs, scale):
                pv_of = {it: n for n, (it, _) in enumerate(pvs)}
                for i in range(len(items) + 3):
                    if i < len(items):
                        g = c.att + i
                        act.wait_ge(biased, g + 1)
                        for qt in range(2):
                            p = prob[:, g % 3, qt, :]
                            e = nc.scalar.activation(p, p, ACT.Exp, bias=nmax[:, g % 3, qt:qt + 1],
                                                     accum_out=rsum[:, g % 3, qt:qt + 1])
                        e.then_inc(expd, 1)
                    if i - 2 in pv_of:
                        n = pv_of[i - 2]
                        act.wait_ge(turned, c.pv + n + 1)
                        if n >= 2:
                            act.wait_ge(attended, c.pv + n - 1)
                        nc.scalar.activation(probT[:, n % 2, :, :], wide[:, 2 + n % 2, :].rearrange("p (k q) -> p k q", k=2),
                                             ACT.Copy).then_inc(turned_copied, 1)

            def forget_gates(norms):
                act.wait_ge(gate_step, 1)
                nc.scalar.activation(forget_z(2), forget_z(1), ACT.Exp, scale=-1.0).then_inc(gate_step, 1)
                act.wait_ge(gate_step, 2)
                nc.scalar.activation(forget_z(2), forget_z(2), ACT.Ln, bias=1.0).then_inc(gate_step, 1)

            def mean_norm(c, nb, per, gate):
                act.wait_ge(mean_off, c.meanb + nb)
                nc.scalar.activation(t1[:, 0:nb, :], cat[:, 0:nb, :], ACT.Square).then_inc(mean_act, 1)
                act.wait_ge(out_evac, state.evac)
                nc.scalar.activation(gate, gate, ACT.Silu).then_inc(mean_act, 1)
                act.wait_ge(mean_sums, 2 * c.mean + 2)
                nc.scalar.activation(t2[:, 0:nb // per, :], wide[:, 0:nb // per, 0:T], ACT.Sqrt, scale=1.0 / (P * per),
                                     bias=eps_col).then_inc(mean_act, 1)

            def gla_gates(norms):
                z, e, l = t1[:, 0:4, :], t1[:, 4:8, :], t1[:, 4:8, :]
                b = t2[:, 0:4, :]
                act.wait_ge(gla_dve, 2)
                nc.scalar.activation(e, z, ACT.Exp, scale=-1.0).then_inc(gla_act, 1)
                act.wait_ge(gla_act, 1)
                nc.scalar.activation(l, e, ACT.Ln, bias=1.0).then_inc(gla_act, 1)
                act.wait_ge(gla_dve, 3)
                nc.scalar.activation(t1[:, 4:8, :], b, ACT.Exp).then_inc(gla_act, 1)
                nc.scalar.activation(work[:, 4:8, :], b, ACT.Exp, scale=-1.0).then_inc(gla_act, 1)
                act.wait_ge(gla_dve, 4)
                nc.scalar.activation(work[:, 0:4, :], work[:, 0:4, :], ACT.Exp).then_inc(gla_act, 1)
                last = b.rearrange("p h t -> p (h t)").rearrange("p (c j) -> p c j", j=64)[:, :, 63]
                nc.scalar.activation(g_decay, last, ACT.Exp).then_inc(gla_act, 1)

            def gla():
                act.wait_ge(gla_mm, 3)
                nc.scalar.activation(g_kdecT.rearrange("p (a b) t -> p a (b t)", a=2), wide[:, 0:2, :], ACT.Copy)\
                    .then_inc(gla_act, 1)

            s.setup, s.first_squares, s.residual, s.ffn_up, s.project = setup, first_squares, residual, ffn_up, project
            s.norm_finish, s.cat_split, s.head_norm, s.attend, s.forget_gates = norm_finish, cat_split, head_norm, attend, forget_gates
            s.mean_norm, s.gla_gates, s.gla = mean_norm, gla_gates, gla
            s.rotate = s.retention = s.band_bias = s.conv = s.tables_2 = lambda *a: None
            order(s)

        @block.vector
        def _(dve):
            s = Stages()
            state = Progress()

            def link(ins):
                state.chain += 1
                ins.then_inc(dve_chain, 1)
                dve.wait_ge(dve_chain, state.chain)

            def split_to(n):
                while state.split < min(n, len(units)):
                    i = state.split
                    u = units[i]
                    dve.wait_ge(w_hi_ready, i + 1)
                    if i >= RING:
                        dve.wait_ge(unit_done, i - RING + 1)
                    nc.vector.tensor_tensor(w_lo[:, i % RING, 0:u.nk, :], raw[:, u.raw % RING, 0:u.nk, P * u.half:P * u.half + P],
                                            w_hi[:, i % RING, 0:u.nk, :].bitcast(F32), ALU.subtract).then_inc(w_lo_ready, 1)
                    state.split += 1

            def setup():
                dve.wait_ge(const_in, 48)
                link(nc.vector.tensor_scalar(gain_col("subln"), gain_col("subln"), 1.0 - LAMBDA_INIT, None, ALU.mult))

            def first_squares(i):
                dve.wait_ge(lam_in, 16)
                lp = prob[:, 0, 0, :].rearrange("p (a b d) -> p a b d", a=2, b=2)
                pr = prob[:, 1, 0, 0:128].rearrange("p (a d) -> p a d", a=2)
                link(nc.vector.tensor_tensor(pr, lp[:, :, 0, :], lp[:, :, 1, :], ALU.mult))
                nc.vector.tensor_reduce(lam_sum, pr, AX.X, ALU.add).then_inc(lam_step, 1)
                dve.wait_ge(pos_in, 16)
                a, n, m = hidf[:, 0, :], hidf[:, 1, :], silu_g[:, 0, :]
                link(nc.vector.tensor_copy(n, pos[:, :]))
                link(nc.vector.tensor_scalar(a, n, rope_freq, None, ALU.mult))
                link(nc.vector.tensor_scalar(n, a, 1.0 / TWO_PI, None, ALU.mult))
                link(nc.vector.tensor_scalar(n, n, ROUND, None, ALU.add))
                link(nc.vector.tensor_scalar(n, n, -ROUND, None, ALU.add))
                for part in TWO_PI_PARTS:
                    link(nc.vector.scalar_tensor_tensor(a, n, -part, a, ALU.mult, ALU.add))
                link(nc.vector.tensor_scalar(m, a, PI, -TWO_PI, ALU.is_gt, ALU.mult))
                link(nc.vector.tensor_tensor(a, a, m, ALU.add))
                link(nc.vector.tensor_scalar(m, a, -PI, TWO_PI, ALU.is_lt, ALU.mult))
                link(nc.vector.tensor_tensor(a, a, m, ALU.add))
                nc.vector.tensor_scalar(a, a, PI, -PI, ALU.min, ALU.max).then_inc(rope_step, 1)
                split_to(RING)
                dve.wait_ge(lam_step, 2)
                link(nc.vector.tensor_tensor(neg_lam, lam_exp[:, 1:2], lam_exp[:, 0:1], ALU.subtract))
                link(nc.vector.tensor_scalar(neg_lam, neg_lam, -LAMBDA_INIT, None, ALU.add))
                dve.wait_ge(rope_step, 3)
                link(nc.vector.tensor_tensor(n, n, n, ALU.mult))
                link(nc.vector.tensor_scalar(rope_c, hidf[:, 1:2, :], -2.0, 1.0, ALU.mult, ALU.add))

            def finish(i, src, gain, kind, need, last=False):
                dve.wait_ge(std_done, i + 1)
                link(nc.vector.reciprocal(t2[:, 1, :], t2[:, 0, :]))
                hi, lo, hi_ready, lo_ready = fills[kind]

                def low(k):
                    dve.wait_ge(hi_ready, 8 * need + k + 1)
                    nc.vector.tensor_tensor(lo[:, k, :], t1[:, k, :], hi[:, k, :].bitcast(F32), ALU.subtract).then_inc(lo_ready, 1)

                for k in range(8):
                    nc.vector.scalar_tensor_tensor(t1[:, k, :], src[:, k, :], gains[:, gain + k:gain + k + 1], t2[:, 1, :],
                                                   ALU.mult, ALU.mult).then_inc(normed, 1)
                    if k and not last:
                        dve.wait_ge(normed, 8 * i + k)
                        low(k - 1)
                if not last:
                    dve.wait_ge(normed, 8 * i + 8)
                    low(7)

            def norm_finish(i, gain, gen, last):
                finish(i, x, gain, "hn", gen, last)

            def cat_split(c):
                for k in range(8):
                    dve.wait_ge(hn_hi_ready, 8 * c.gen + k + 1)
                    nc.vector.tensor_tensor(hn_lo[:, k, :], cat[:, k, :], hn_hi[:, k, :].bitcast(F32), ALU.subtract)\
                        .then_inc(hn_lo_ready, 1)

            def project(name):
                l = lin[name]
                for i in range(l.u0, l.u1):
                    o = units[i].out
                    dve.wait_ge(unit_done, i + 1)
                    nc.vector.tensor_copy(dest_ap(name, o - l.o0), out_ap(o, units[i].mode)).then_inc(out_evac, 1)
                    split_to(i + RING + 1)

            def residual(name, scale, i):
                l = lin[name]
                for n in range(l.u0, l.u1):
                    u = units[n]
                    if u.last:
                        k = u.out - l.o0
                        dve.wait_ge(unit_done, n + 1)
                        nc.vector.scalar_tensor_tensor(x[:, k, :], out_ap(u.out, "F"), scale, x[:, k, :],
                                                       ALU.mult, ALU.add).then_inc(out_evac, 1)
                    split_to(n + RING + 1)
                dve.wait_ge(out_evac, freed[l.o1 - 1][1])

            def ffn_up(f, n, mi, gain, gen):
                l = lin[f"up{f}"]

                def mul(h):
                    dve.wait_ge(unit_done, u0 + 2 + h + 1)
                    dve.wait_ge(gate_evac, m0 + h + 1)
                    if m0:
                        dve.wait_ge(hid_hi_ready, m0 - 1 + h)
                        dve.wait_ge(hid_lo_ready, m0 - 1 + h)
                    nc.vector.tensor_tensor(hidf[:, h, :], silu_g[:, h, :], acc[:, units[u0 + 2 + h].out % BANKS, 0:T],
                                            ALU.mult).then_inc(hid_mul, 1)

                def low(h):
                    dve.wait_ge(hid_hi_ready, m0 + h + 1)
                    dve.wait_ge(hid_mul, m0 + h + 1)
                    nc.vector.tensor_tensor(hid_lo[:, 2 * ch + h, :], hidf[:, h, :], hid_hi[:, 2 * ch + h, :].bitcast(F32),
                                            ALU.subtract).then_inc(hid_lo_ready, 1)

                for ch in range(FF // CW):
                    u0, m0 = l.u0 + 4 * ch, HB * f + 2 * ch
                    split_to(u0 + RING + 1)
                    split_to(u0 + RING + 2)
                    mul(0)
                    split_to(u0 + RING + 3)
                    low(0)
                    mul(1)
                    split_to(u0 + RING + 4)
                    low(1)
                    if n is not None and ch == 3:
                        finish(mi, keep, gain, "mn", n)

            def head_norm(c, src, nb, per, gain):
                dve.wait_ge(head_std, c.head + 1)
                ns = nb // 2 if per == 256 else nb
                link(nc.vector.reciprocal(t2[:, 0:ns, :], t2[:, 0:ns, :]))
                for b in range(nb):
                    r = t2[:, b // 2 if per == 256 else b, :]
                    ins = nc.vector.scalar_tensor_tensor(src[:, b, :], src[:, b, :], gain_col(gain[b]), r, ALU.mult, ALU.mult)
                ins.then_inc(head_normed, 1)

            def rotate(c, src, perm, cs, sn):
                if c.rot == 0:
                    dve.wait_ge(head_normed, c.head)
                elif c.rot == 4:
                    dve.wait_ge(tables_in, 16 * 3)
                    dve.wait_ge(out_evac, freed[lin["ev"].o1 - 1][1])
                for b in range(4):
                    pair = src[:, 2 * b:2 * b + 2, :]
                    dve.wait_ge(rot_done, c.rot + b + 1)
                    nc.vector.tensor_tensor(t1[:, 2 * b:2 * b + 2, :], wide[:, b, :].rearrange("p (a t) -> p a t", a=2),
                                            sn.to_broadcast([P, 2, T]), ALU.mult)
                    ins = nc.vector.tensor_tensor(pair, pair, cs.to_broadcast([P, 2, T]), ALU.mult)
                link(ins)
                for b in range(4):
                    pair = src[:, 2 * b:2 * b + 2, :]
                    nc.vector.tensor_tensor(pair, pair, t1[:, 2 * b:2 * b + 2, :], ALU.add).then_inc(rot_added, 1)

            def attend(c, items, pvs, scale):
                pv_of = {it: n for n, (it, _) in enumerate(pvs)}
                blocks = sorted({b for _, l in pvs for _, b, _ in l})
                last_of = {b: n for n, (_, l) in enumerate(pvs) for _, b, _ in l}
                bias0 = items[0][2]
                if bias0 is not None:
                    dve.wait_ge(masks_in, 32)
                    if c.head == 6:
                        dve.wait_ge(band_masked, 8)
                for i in range(len(items) + 5):
                    if i < len(items):
                        g = c.att + i
                        bias = items[i][2]
                        dve.wait_ge(scores, g + 1)
                        if i - 3 in pv_of:
                            dve.wait_ge(turned, c.pv + pv_of[i - 3] + 1)
                        if i >= 2:
                            dve.wait_ge(probs, g - 1)
                        src = wide[:, i % 2, :].rearrange("p (q k) -> p q k", q=2)
                        if bias is None:
                            link(nc.vector.tensor_scalar(prob[:, g % 3, :, :], src, scale, None, ALU.mult))
                        else:
                            link(nc.vector.scalar_tensor_tensor(prob[:, g % 3, :, :], src, scale, bias, ALU.mult, ALU.add))
                        nc.vector.tensor_reduce(nmax[:, g % 3, :], prob[:, g % 3, :, :], AX.X, ALU.max, negate=True)\
                            .then_inc(biased, 1)
                    if 1 <= i <= len(items):
                        g = c.att + i - 1
                        partner = items[i - 1][4]
                        dve.wait_ge(expd, g + 1)
                        link(nc.vector.reciprocal(rinv[:, g % 3, :], rsum[:, g % 3, :]))
                        p = prob[:, g % 3, :, :]
                        if partner is None:
                            nc.vector.tensor_tensor(p, p, rinv[:, g % 3, :].unsqueeze(2).to_broadcast([P, 2, T]), ALU.mult)\
                                .then_inc(probs, 1)
                        else:
                            link(nc.vector.tensor_scalar(rinv_lam, rinv[:, g % 3, :], neg_lam, None, ALU.mult))
                            dve.wait_ge(probs, g)
                            for qt in range(2):
                                ins = nc.vector.scalar_tensor_tensor(p[:, qt, :], p[:, qt, :], rinv_lam[:, qt:qt + 1],
                                                                     prob[:, (g - 1) % 3, qt, :], ALU.mult, ALU.add)
                            ins.then_inc(probs, 1)
                    if i - 4 in pv_of:
                        n = pv_of[i - 4]
                        for _, b, _ in pvs[n][1]:
                            if last_of[b] == n:
                                dve.wait_ge(attended, c.pv + n + 1)
                                nc.vector.tensor_copy(cat[:, b, :], acc[:, blocks.index(b) % 4, 0:T]).then_inc(att_out, 1)

            def forget_gates(norms):
                dve.wait_ge(gate_mm, 1)
                z, a, e, f = (forget_z(i) for i in range(4))
                link(nc.vector.tensor_scalar(z, wide[0:8, 1, 0:T], gain_col("fb")[0:8], None, ALU.add))
                link(nc.vector.tensor_scalar(a, z, -1.0, None, ALU.mult))
                nc.vector.tensor_tensor(a, a, z, ALU.max).then_inc(gate_step, 1)
                dve.wait_ge(gate_step, 3)
                link(nc.vector.scalar_tensor_tensor(f, z, 0.0, e, ALU.min, ALU.subtract))
                link(nc.vector.memset(a, 1.0))
                link(nc.vector.tensor_tensor_scan(z, a, f, 0.0, ALU.mult, ALU.add))
                nc.vector.tensor_scalar(cum, z, 8.0, None, ALU.mult)
                nc.vector.tensor_scalar(ncum, z, -8.0, None, ALU.mult).then_inc(gate_step, 1)

            def band_bias():
                for h in range(8):
                    dve.wait_ge(band_turned, h + 1)
                    for qt in range(2):
                        ins = nc.vector.tensor_tensor(band(h)[:, qt, :], wide[:, h % 4, T * (1 - qt):T * (1 - qt) + T],
                                                      chunked_odd[:, qt, :], ALU.add)
                    ins.then_inc(band_masked, 1)

            def conv():
                cb, cc, ch, y = work[:, 24:28, :], work[:, 28:32, :], work[:, 32:36, :], t1[:, 0:4, :]
                w = gains[:, GC["conv"]:GC["conv"] + 12]
                dve.wait_ge(out_evac, freed[lin["dv"].o1 - 1][1])
                link(nc.vector.tensor_tensor(ch, cc, ch, ALU.mult))
                for b in range(4):
                    ins = nc.vector.tensor_scalar(y[:, b, :], ch[:, b, :], w[:, 8 + b:9 + b], None, ALU.mult)
                link(ins)
                for back in (1, 2):
                    for b in range(4):
                        j = 4 * (2 - back) + b
                        ins = nc.vector.scalar_tensor_tensor(y[:, b, back:T], ch[:, b, 0:T - back], w[:, j:j + 1],
                                                             y[:, b, back:T], ALU.mult, ALU.add)
                    link(ins)
                nc.vector.tensor_tensor(cat[:, 0:4, :], cb, y, ALU.mult).then_inc(conv_done, 1)

            def retention():
                for h in range(5):
                    if h < 4:
                        dve.wait_ge(ret_s, h + 1)
                        if h >= 2:
                            dve.wait_ge(ret_o, h - 1)
                        nc.vector.tensor_tensor(probT[:, h % 2, :, :], wide[:, h % 2, :].rearrange("p (k q) -> p k q", k=2),
                                                decay[:, h, :, :], ALU.mult).then_inc(ret_p, 1)
                    if h:
                        dve.wait_ge(ret_o, h)
                        nc.vector.tensor_copy(cat[:, h - 1, :], acc[:, h - 1, 0:T]).then_inc(ret_copied, 1)

            def mean_norm(c, nb, per, gate):
                dve.wait_ge(mean_sums, 2 * c.mean + 1)
                if c.mean == 0:
                    dve.wait_ge(ret_copied, 4)
                else:
                    dve.wait_ge(gla_dve, 26)
                for b in range(nb):
                    nc.vector.scalar_tensor_tensor(cat[:, b, :], wide[:, b // per, 0:T], -1.0 / (P * per), cat[:, b, :],
                                                   ALU.mult, ALU.add).then_inc(mean_off, 1)
                dve.wait_ge(mean_act, 3 * c.mean + 3)
                link(nc.vector.reciprocal(t2[:, 0:nb // per, :], t2[:, 0:nb // per, :]))
                for b in range(nb):
                    ins = nc.vector.tensor_tensor(cat[:, b, :], cat[:, b, :], t2[:, b // per, :], ALU.mult)
                link(ins)
                for b in range(nb):
                    nc.vector.tensor_tensor(cat[:, b, :], cat[:, b, :], gate[:, b, :], ALU.mult).then_inc(mean_normed, 1)

            def gla_gates(norms):
                dve.wait_ge(gla_mm, 1)
                nc.vector.tensor_copy(t2[0:16, 6, :], wide[0:16, 1, 0:T]).then_inc(gla_dve, 1)
                dve.wait_ge(gla_mm, 2)
                z, a, l, b = work[:, 0:4, :], t1[:, 0:4, :], t1[:, 4:8, :], t2[:, 0:4, :]
                for h in range(4):
                    ins = nc.vector.tensor_scalar(z[:, h, :], wide[:, h, 0:T], gain_col(("ba", h)), None, ALU.add)
                link(ins)
                link(nc.vector.tensor_scalar(a, z, -1.0, None, ALU.mult))
                nc.vector.tensor_tensor(a, a, z, ALU.max).then_inc(gla_dve, 1)
                dve.wait_ge(gla_act, 2)
                flat = lambda v: v.rearrange("p h t -> p (h t)")
                link(nc.vector.scalar_tensor_tensor(flat(z), flat(z), 0.0, flat(l), ALU.min, ALU.subtract))
                link(nc.vector.tensor_scalar(z, z, 1.0 / 16.0, None, ALU.mult))
                link(nc.vector.memset(a, 1.0))
                link(nc.vector.memset(flat(a).rearrange("p (c j) -> p c j", j=64)[:, :, 0:1], 0.0))
                nc.vector.tensor_tensor_scan(flat(b), flat(a), flat(z), 0.0, ALU.mult, ALU.add).then_inc(gla_dve, 1)
                dve.wait_ge(gla_dve, 3)
                chunks = flat(b).rearrange("p (c j) -> p c j", j=64)
                nc.vector.tensor_tensor(flat(z).rearrange("p (c j) -> p c j", j=64), chunks[:, :, 63:64].to_broadcast([P, 16, 64]),
                                        chunks, ALU.subtract).then_inc(gla_dve, 1)

            def gla():
                dve.wait_ge(out_evac, freed[lin["gr"].o1 - 1][1])
                dve.wait_ge(gla_act, 6)
                flat = lambda v: v.rearrange("p h t -> p (h t)")
                nc.vector.scalar_tensor_tensor(flat(g_q), flat(g_q), float(P) ** -0.5, flat(t1[:, 4:8, :]), ALU.mult, ALU.mult)
                link(nc.vector.tensor_tensor(g_kdec, g_k, work[:, 0:4, :], ALU.mult))
                nc.vector.tensor_tensor(g_k, g_k, work[:, 4:8, :], ALU.mult).then_inc(gla_dve, 1)
                link(nc.vector.memset(g_scores, 0.0))
                dve.wait_ge(gla_mm, 4)
                for r in range(2):
                    rows = slice(64 * r, 64 * r + 64)
                    ins = nc.vector.tensor_tensor(g_scores[rows, :, r::2, :].rearrange("p h c q -> p (h c) q"),
                                                  wide[rows, 2, :].rearrange("p (a q) -> p a q", q=64),
                                                  key_before[rows].unsqueeze(1).to_broadcast([64, 8, 64]), ALU.mult)
                ins.then_inc(gla_dve, 1)
                for n in range(3):
                    for h in range(4):
                        dve.wait_ge(gla_mm, 5 + 4 * n + h)
                        if n == 0:
                            ins = nc.vector.tensor_copy(g_state[:, 0, h, :], acc[:, h, 0:T])
                        else:
                            dve.wait_ge(gla_dve, 6 + 4 * (n - 1) + h + 1)
                            ins = nc.vector.scalar_tensor_tensor(g_state[:, n, h, :], g_state[:, n - 1, h, :],
                                                                 g_decay[:, 4 * h + n:4 * h + n + 1], acc[:, h, 0:T],
                                                                 ALU.mult, ALU.add)
                        ins.then_inc(gla_dve, 1)
                for b in range(8):
                    dve.wait_ge(gla_mm, 17 + b)
                    nc.vector.tensor_copy(cat[:, b, :], acc[:, b % 4, 0:T]).then_inc(gla_dve, 1)

            s.setup, s.first_squares, s.residual, s.ffn_up, s.project = setup, first_squares, residual, ffn_up, project
            s.norm_finish, s.cat_split, s.head_norm, s.attend, s.forget_gates = norm_finish, cat_split, head_norm, attend, forget_gates
            s.rotate, s.conv, s.retention, s.mean_norm, s.gla_gates, s.gla = rotate, conv, retention, mean_norm, gla_gates, gla
            s.band_bias, s.tables_2 = band_bias, lambda *a: None
            order(s)

        @block.gpsimd
        def _(pool):
            pool.dma_start(prob[:, 0, 0, :], io["lam"].partition_broadcast(P)).then_inc(lam_in, 16)
            pool.dma_start(pos[:, :], io["positions"].partition_broadcast(P)).then_inc(pos_in, 16)
            pool.dma_start(keep[:, 0:8, :], io["mem"].rearrange("(k p) t -> p k t", p=P)).then_inc(mem_in, 16)
            pool.dma_start(causal, io["masks"][:, 0:2, :]).then_inc(masks_in, 16)
            pool.dma_start(chunked, io["masks"][:, 2:4, :]).then_inc(masks_in, 16)
            pool.dma_start(small_w[:, :, 0:8], io["wf"].rearrange("(k p) n -> p k n", p=P)).then_inc(wf_in, 16)
            pool.wait_ge(hn_lo_ready, 8 * 5)
            pool.wait_ge(unit_done, lin["up1"].u0 + 1)
            pool.dma_start(keep[:, 0:8, :], io["mem"].rearrange("(k p) t -> p k t", p=P)).then_inc(mem_in, 16)
            pool.wait_ge(unit_done, lin["down2"].u1)
            pool.dma_start(chunked_odd, io["masks"][:, 2:4, :]).then_inc(band_in, 16)
            for h in range(8):
                b = io["band"]
                skew = bass.AP(b.tensor, 512 * h, [[1, P], [P, 2], [1, T]])
                pool.dma_start(band(h), skew).then_inc(band_in, 16)
            pool.wait_ge(unit_done, lin["down4"].u1)
            pool.dma_start(work[:, 0:4, :], io["rotations"]).then_inc(tables_in, 16)
            pool.dma_start(dil_bias, io["masks"][:, 4:6, :]).then_inc(tables_in, 16)
            pool.dma_start(keep[:, 8:16, :], io["decay"]).then_inc(tables_in, 16)
            pool.wait_ge(unit_done, lin["down6"].u1)
            pool.dma_start(small_w[:, :, :], io["wa"].rearrange("(k p) n -> p k n", p=P)).then_inc(wa_in, 16)
            pool.dma_start(wa2[:, :], io["wa2"]).then_inc(wa_in, 16)


PI = float(np.float32(np.pi))
TWO_PI = 2.0 * float(np.pi)
TWO_PI_PARTS = (6.28125, 1014 * 2.0 ** -19, TWO_PI - 6.28125 - 1014 * 2.0 ** -19)
ROUND = 1.5 * 2.0 ** 23


def constants():
    f32 = np.float32
    p = np.arange(P)
    mats = np.zeros((P, 7, P), f32)
    mats[:, 0] = np.eye(P)
    mats[:, 1] = 1.0
    mats[:, 2] = (p[:, None] // 64) == (p[None, :] // 64)
    for m in range(P):
        if m % 64 < 8:
            mats[m + 8, 3, m] = -1.0
        elif m % 64 < 16:
            mats[m - 8, 3, m] = 1.0
        mats[(m + 64) % P, 4, m] = -1.0 if m < 64 else 1.0
    mats[:, 6] = np.eye(P)[::-1]
    mats[:, 5, 0:64] = (p[:, None] % 64) <= np.arange(64)[None, :]
    rope = f32(500000.0) ** (-np.arange(0, 16, 2, dtype=f32) / f32(16))
    cols = np.zeros((P, 4), f32)
    cols[:, 0] = EPS
    for m in range(P):
        if m % 64 < 16:
            cols[m, 1] = rope[m % 8]
    t = np.arange(T)
    q, k = t[:, None], t[None, :]
    off = f32(-1e30)
    count = ((q >= k) & (q - k <= 128)) * 1.0 + ((q >= k) & ((q - k) % 4 == 0)) + ((q >= k) & ((q - k) % 16 == 0))
    kinds = [np.where(q >= k, f32(0), off), np.where(q // 64 >= k // 64, f32(0), off),
             np.where(count > 0, np.log(np.maximum(count, 1.0)), off)]
    masks = np.concatenate([m.astype(f32).reshape(2, P, T).transpose(1, 0, 2) for m in kinds], axis=1)
    decay = np.zeros((P, 8, T), f32)
    for h in range(4):
        g = 1.0 - 2.0 ** (-5.0 - h)
        d = np.where(k >= q, g ** np.maximum(k - q, 0), 0.0) * P ** -0.5
        decay[:, 2 * h:2 * h + 2] = d.reshape(2, P, T).transpose(1, 0, 2)
    freq = f32(10000.0) ** (-np.linspace(0.0, 1.0, 64, dtype=f32))
    ret = t.astype(f32)[None, :] * freq[p % 64][:, None]
    dil = t.astype(f32)[None, :] * cols[:, 1:2]
    rot = np.stack([np.cos(ret), np.sin(ret), np.cos(dil), np.sin(dil)], axis=1).astype(f32)
    return {"mats": mats, "cols": cols, "masks": np.ascontiguousarray(masks), "decay": decay, "rotations": rot}


def lay_out(inputs):
    GC, NG = gain_columns()
    gains = np.zeros((P, NG), np.float32)

    def put(name, v):
        gains[:, GC[name]:GC[name] + v.shape[1]] = v

    def blocks(v):
        return v.reshape(-1, P).T

    def twice(v):
        return np.concatenate([v, v], axis=-1).T

    for l in range(2):
        for j in range(5):
            put(f"ln{l}{j}", blocks(inputs["ln_gains"][l, j]))
        put(f"pre{l}", blocks(inputs["ffn_pre_norm_2"][l]))
        put(f"mix{l}", blocks(inputs["mix_norm_2"][l]))
        put(f"post{l}", blocks(inputs["ffn_post_norm_2"][l]))
        put(f"x{l}", blocks(inputs["x_qk_gains"][l]))
    put("final", blocks(inputs["final_norm_2"]))
    put("even", twice(inputs["even_qk_gains"][0]))
    put("odd", twice(inputs["odd_qk_gains"][0]))
    put("subln", blocks(inputs["even_subln_gain"][0]))
    put("conv", blocks(inputs["odd_conv_w"][0]))
    put("ba", blocks(inputs["gla_b_a_2"][0]))
    gains[0:8, GC["fb"]] = inputs["even_f_bias"][0]
    rel = inputs["odd_rel_bias"][0][:, ::-1]
    band = np.concatenate([np.repeat(rel[:, 0:1], 127, axis=1), rel, np.repeat(rel[:, 256:257], 128, axis=1)], axis=1)
    return {"x": np.ascontiguousarray(inputs["x"][0].T), "mem": np.ascontiguousarray(inputs["mem"][0].T), "gains": gains,
            "positions": inputs["positions"], "lam": inputs["even_lambda"].reshape(1, 256),
            "wf": np.ascontiguousarray(inputs["even_w_in"][0][:, 1536:1544]),
            "wa": np.ascontiguousarray(inputs["gla_w_in_2"][0][:, 3072:3088]), "wa2": inputs["gla_w_a2_2"][0],
            "band": np.ascontiguousarray(band)}


_WEIGHTS = ["ffn1_w_in", "ffn1_w_out", "ffn2_w_in", "ffn2_w_out", "even_w_in", "even_w_out", "odd_w_in", "odd_w_out",
            "x_w_q", "x_w_kv", "x_w_o", "ffn_pre_w_gate_2", "ffn_pre_w_up_2", "ffn_pre_w_down_2", "ab_w_in_2",
            "ab_w_out_2", "gla_w_in_2", "gla_w_out_2", "ffn_post_w_gate_2", "ffn_post_w_up_2", "ffn_post_w_down_2"]


def kernel(**inputs):
    import concourse.bacc as _bacc
    from concourse.bass_utils import run_bass_kernel_spmd as _run

    inputs = {k: np.asarray(v) for k, v in inputs.items()}
    arrays = {**lay_out(inputs), **constants(), **{n: inputs[n] for n in _WEIGHTS}}
    arrays = {f"in_{k}": np.ascontiguousarray(v) for k, v in arrays.items()}
    nc = _bacc.Bacc("TRN2", target_bir_lowering=False, num_devices=1)
    io = {k[3:]: nc.dram_tensor(k, a.shape, mybir.dt.from_np(a.dtype), kind="ExternalInput").ap() for k, a in arrays.items()}
    out = nc.dram_tensor("out", (D, T), F32, kind="ExternalOutput").ap()
    build(nc, io, out)
    r = _run(nc, [arrays], core_ids=[0])
    return np.ascontiguousarray(r.results[0]["out"].T)[None]
```

```python
from collections import namedtuple
from contextlib import ExitStack

import numpy as np

import concourse.bass as bass
from concourse import mybir

F32 = mybir.dt.float32
F32R = mybir.dt.float32r
I32 = mybir.dt.int32
ALU = mybir.AluOpType
ACT = mybir.ActivationFunctionType
AX = mybir.AxisListType

P = 128
T = 256
D = 1024
KB = D // P
FF = 2816
HB = FF // P
CW = 256
EPS = 1e-6
MEM_NORMS = 2
LAMBDA_INIT = 0.8 - 0.6 * float(np.exp(-0.0))
GATE, UP, OTHER = range(3)
RING = 4
BANKS = 4



class Stages:
    pass


class Progress:

    def __init__(self):
        self.split = self.evac = self.chain = 0
        self.sums = None


class Counts:

    def __init__(self):
        self.norm = 0
        self.gen = 0
        self.fill = 0
        self.head = 0
        self.rot = 0
        self.att = 0
        self.pv = 0
        self.group = 0
        self.conv = 0
        self.mean = 0
        self.meanb = 0


Unit = namedtuple("Unit", "raw half k0 nk first last out mode src need slot free held")
VALUES = ("av", "bv", "dv", "rv", "ev", "gv")
Linear = namedtuple("Linear", "u0 u1 o0 o1")


def gain_columns():
    at, n = {}, 0
    for name, width in ([(f"ln{l}{j}", 8) for l in range(2) for j in range(5)]
                        + [("pre0", 8), ("pre1", 8), ("mix0", 8), ("mix1", 8), ("post0", 8), ("post1", 8), ("final", 8)]
                        + [("even", 4), ("odd", 2), ("subln", 1), ("x0", 4), ("x1", 4), ("conv", 12),
                           ("ba", 4), ("fb", 1)]):
        at[name] = n
        n += width
    return at, n


def plan_stream(io):
    loads, units, outs, lin = [], [], [], {}

    slot, holder = 0, [None] * RING

    def add(name, chunks, rows, mode, src, need, frees=lambda c: OTHER, width=CW):
        nonlocal slot
        u0, o0, halves = len(units), len(outs), width // P
        for c, (w, col) in enumerate(chunks):
            if mode == "T" and slot % 2:
                slot = (slot + 1) % RING
            for k0 in range(0, rows, 8):
                nk = min(8, rows - k0)
                loads.append((w[k0 * P:(k0 + nk) * P, col:col + width].rearrange("(k p) n -> p k n", p=P), nk, width))
                for half in range(halves):
                    out = o0 + halves * c + half
                    first, last = k0 == 0, k0 + nk == rows
                    if last:
                        outs.append((len(units), frees(c)))
                    i = len(units)
                    units.append(Unit(len(loads) - 1, half, k0, nk, first, last, out, mode, src,
                                      need if src != "hid" else HB * need + k0 + nk, slot, holder[slot],
                                      i + 2 if mode == "T" and half == 0 else i + 1))
                    holder[slot] = units[-1].held
                    slot = (slot + 1) % RING
        lin[name] = Linear(u0, len(units), o0, len(outs))

    def cols(w, c0, n):
        return [(w, c0 + c) for c in range(0, n, CW)]

    gen, fill = 0, 0

    def ffn(f, gu, wo):
        nonlocal gen
        add(f"up{f}", gu, KB, "F", "hn", gen, lambda c: UP if c % 2 else GATE)
        add(f"down{f}", cols(wo, 0, D), HB, "F", "hid", f)
        gen += 1

    def project(w, *parts):
        for name, c0, width in parts:
            add(name, cols(w, c0, width), KB, "T" if name in VALUES else "F", "hn", gen)

    for n in range(2):
        def fused(w):
            return [x for c in range(0, FF, CW) for x in ((w, c), (w, FF + c))]

        kv = io["x_w_kv"][n]
        ffn(2 * n, fused(io["ffn1_w_in"][n]), io["ffn1_w_out"][n])
        if n == 0:
            w, wo = io["even_w_in"][0], io["even_w_out"][0]
            project(w, ("aq", 0, 512), ("ak", 512, 512), ("av", 1024, 512))
            add("af", [(w, 1536)], KB, "F", "hn", gen, width=P)
            add("memk0", cols(kv, 0, D), KB, "F", "mn", fill)
            project(w, ("bq", 1544, 512), ("bk", 2056, 512), ("bv", 2568, 512))
        else:
            w, wo = io["odd_w_in"][0], io["odd_w_out"][0]
            project(w, ("dq", 1536, 512), ("dk", 2048, 512), ("dv", 2560, 512))
            add("memk1", cols(kv, 0, D), KB, "F", "mn", fill)
            project(w, ("cb", 0, 512), ("cc", 512, 512), ("ch", 1024, 512))
        add(f"memv{n}", cols(kv, D, D), KB, "T", "mn", fill)
        gen, fill = gen + 1, fill + 1
        add(f"mixout{n}", cols(wo, 0, D), KB, "F", "mn", fill)
        fill += 1
        project(io["x_w_q"][n], (f"xq{n}", 0, D))
        gen += 1
        add(f"xo{n}", cols(io["x_w_o"][n], 0, D), KB, "F", "mn", fill)
        fill += 1
        ffn(2 * n + 1, fused(io["ffn2_w_in"][n]), io["ffn2_w_out"][n])
    for n in range(2):
        def paired(a, b):
            return [x for c in range(0, FF, CW) for x in ((a, c), (b, c))]

        ffn(4 + 2 * n, paired(io["ffn_pre_w_gate_2"][n], io["ffn_pre_w_up_2"][n]), io["ffn_pre_w_down_2"][n])
        if n == 0:
            w, wo = io["ab_w_in_2"][0], io["ab_w_out_2"][0]
            project(w, *((name, 512 * i, 512) for i, name in enumerate(("rq", "rk", "rv", "rg", "eq", "ek", "ev"))))
        else:
            w, wo = io["gla_w_in_2"][0], io["gla_w_out_2"][0]
            add("ga", [(w, 2960)], KB, "F", "hn", gen, width=P)
            project(w, ("gq", 0, 512), ("gk", 512, 512), ("gv", 1024, 1024), ("gr", 2048, 1024))
        gen += 1
        add(f"mixout{2 + n}", cols(wo, 0, D), KB, "F", "mn", fill)
        fill += 1
        ffn(5 + 2 * n, paired(io["ffn_post_w_gate_2"][n], io["ffn_post_w_up_2"][n]), io["ffn_post_w_down_2"][n])
    return loads, units, outs, lin


def build(nc, io, out):
    loads, units, outs, lin = plan_stream(io)
    GC, NG = gain_columns()
    freed, count = [], [0, 0, 0]
    for _, kind in outs:
        count[kind] += 1
        freed.append((kind, count[kind]))
    last_of_load = {u.raw: i for i, u in enumerate(units)}
    last_reader = {}
    for i, u in enumerate(units):
        if u.src != "hid":
            last_reader[u.src, u.need] = i
    last_hid_reader = [lin[f"down{f}"].u1 - 1 for f in range(8)]

    with ExitStack() as ctx:
        def sb(name, shape, dt=F32):
            return ctx.enter_context(nc.sbuf_tensor(name, shape, dt))

        def sem(name):
            return ctx.enter_context(nc.semaphore(name))

        x = sb("x", [P, KB, T])
        hn_hi = sb("hn_hi", [P, KB, T], F32R)
        hn_lo = sb("hn_lo", [P, KB, T], F32R)
        mn_hi = sb("mn_hi", [P, KB, T], F32R)
        mn_lo = sb("mn_lo", [P, KB, T], F32R)
        raw = sb("raw", [P, RING, 8, CW])
        w_hi = sb("w_hi", [P, RING, 8, P], F32R)
        w_lo = sb("w_lo", [P, RING, 8, P], F32R)
        t1 = sb("t1", [P, KB, T])
        t2 = sb("t2", [P, KB, T])
        keep = sb("keep", [P, 16, T])
        prob = sb("prob", [P, 3, 2, T])
        probT = sb("probT", [P, 2, 2, T])
        gains = sb("gains", [P, NG])
        mats = sb("mats", [P, 7, P])
        colc = sb("colc", [P, 4])
        silu_g = sb("silu_g", [P, 2, T])
        hidf = sb("hidf", [P, 2, T])
        small = sb("small", [P, 64])
        rstd = sb("rstd", [P, 2, T])
        wa2 = sb("wa2", [P, 512])
        pos = sb("pos", [P, T], I32)
        with nc.sbuf_tensor("hid_hi", [P, HB, T], F32R) as hid_hi, nc.sbuf_tensor("hid_lo", [P, HB, T], F32R) as hid_lo:
            pass
        work = sb("work", [P, 2 * HB, T])
        ident, ones, ones64, perm_rope, perm_ret = (mats[:, i, :] for i in range(5))
        reverse = mats[:, 6, :]
        key_before = mats[:, 5, 0:64]
        eps_col, rope_freq = colc[:, 0:1], colc[:, 1:2]

        acc = ctx.enter_context(nc.psum_tensor("acc", [P, BANKS, 512], F32))
        wide = ctx.enter_context(nc.psum_tensor("wide", [P, 4, 512], F32))

        raw_in = [sem(f"raw_in{i}") for i in range(RING)]
        w_hi_ready, w_lo_ready, unit_done = sem("w_hi_ready"), sem("w_lo_ready"), sem("unit_done")
        gate_evac, out_evac = sem("gate_evac"), sem("out_evac")
        hn_hi_ready, hn_lo_ready = sem("hn_hi_ready"), sem("hn_lo_ready")
        mn_hi_ready, mn_lo_ready = sem("mn_hi_ready"), sem("mn_lo_ready")
        silu_done, hid_mul, hid_hi_ready, hid_lo_ready = sem("silu_done"), sem("hid_mul"), sem("hid_hi_ready"), sem("hid_lo_ready")
        squares_added = sem("squares_added")
        squares, sums_done, std_done, normed = sem("squares"), sem("sums_done"), sem("std_done"), sem("normed")
        const_in, mats_in, mem_in, x_in = sem("const_in"), sem("mats_in"), sem("mem_in"), sem("x_in")
        dve_chain, act_chain, pool_chain = sem("dve_chain"), sem("act_chain"), sem("pool_chain")
        head_sq, head_sums, head_std, head_normed = sem("head_sq"), sem("head_sums"), sem("head_std"), sem("head_normed")
        rot_done, rot_added = sem("rot_done"), sem("rot_added")
        scores, biased, expd, probs, turned, turned_copied = (
            sem("scores"), sem("biased"), sem("expd"), sem("probs"), sem("turned"), sem("turned_copied"))
        attended, att_out = sem("attended"), sem("att_out")
        masks_in, pos_in, lam_in, wa_in, tables_in = (
            sem("masks_in"), sem("pos_in"), sem("lam_in"), sem("wa_in"), sem("tables_in"))
        gate_step = sem("gate_step")
        rope_step = sem("rope_step")
        lam_step = sem("lam_step")
        conv_done = sem("conv_done")
        ret_s, ret_p, ret_o, ret_copied = sem("ret_s"), sem("ret_p"), sem("ret_o"), sem("ret_copied")
        gla_mm, gla_dve, gla_act = sem("gla_mm"), sem("gla_dve"), sem("gla_act")
        mean_off, mean_sums, mean_act, mean_normed = sem("mean_off"), sem("mean_sums"), sem("mean_act"), sem("mean_normed")
        final_out = sem("final_out")
        band_in, band_turned, band_masked = sem("band_in"), sem("band_turned"), sem("band_masked")

        memk_out = work[:, 0:8, :]
        memv = work[:, 8:16, :].rearrange("p b t -> p (b t)").rearrange("p (i n) -> p i n", i=2)
        cat = keep[:, 0:8, :]

        def vals(a, nb):
            return work[:, a:a + nb, :].rearrange("p b t -> p (b t)").rearrange("p (i n) -> p i n", i=2)

        dest = {"aq": 16, "ak": 20, "bq": 24, "bk": 28, "av": 32, "bv": 36,
                "dq": 16, "dk": 20, "cb": 24, "cc": 28, "ch": 32, "dv": 36,
                "rq": 16, "rk": 20, "rg": 24, "eq": 28, "ek": 32, "rv": 36, "ev": 40,
                "gq": 16, "gk": 20, "gr": 24, "gv": 32,
                "memk0": 0, "memk1": 0, "memv0": 8, "memv1": 8, "xq0": 16, "xq1": 16}
        nblk = {n: (lin[n].o1 - lin[n].o0) for n in dest}

        causal, chunked = keep[:, 8:10, :], keep[:, 10:12, :]
        rope_c, rope_s = keep[:, 12:13, :], keep[:, 13:14, :]
        dil_bias = work[:, 4:6, :]
        chunked_odd = work[:, 40:42, :]
        ret_c, ret_sn = work[:, 0:1, :], work[:, 1:2, :]
        dil_c, dil_sn = work[:, 2:3, :], work[:, 3:4, :]
        decay = keep[:, 8:16, :].rearrange("p (h k) t -> p h k t", h=4)

        def band(h):
            return work[:, 8 + 2 * h:10 + 2 * h, :] if h < 4 else keep[:, 8 + 2 * (h - 4):10 + 2 * (h - 4), :]

        cum, ncum = keep[0:8, 14, :], keep[0:8, 15, :]

        def half(a, h):
            return work[64 * (h % 2):64 * (h % 2) + 64, a + h // 2, :]

        def attention(kind):

            def halves(v, b0):
                return [(h, [(v[:, :, 64 * h:64 * h + 64], 0, 64 * (h % 2))], [b0 + h // 2] if h % 2 else []) for h in range(8)]

            if kind == "A":
                return ([([half(16, h)], [half(20, h)], causal, h, None) for h in range(8)], halves(vals(32, 4), 0), 0.125)
            if kind == "B":
                v = vals(36, 4)
                return ([([half(24, i)], [half(28, i)], chunked, None, i - 1 if i % 2 else None) for i in range(8)],
                        [(2 * h + 1, [(v[:, :, P * h:P * h + P], 0, 0)], [4 + h]) for h in range(4)], 0.125)
            if kind == "D":
                return ([([half(16, h)], [half(20, h)], band(h), None, None) for h in range(8)], halves(vals(36, 4), 4), 0.125)
            if kind == "E":
                return ([([half(28, h)], [half(32, h)], dil_bias, None, None) for h in range(8)], halves(vals(40, 4), 4), 0.125)
            return ([([work[:, 16 + 2 * h, :], work[:, 17 + 2 * h, :]], [work[:, 2 * h, :], work[:, 2 * h + 1, :]],
                      None, None, None) for h in range(4)],
                    [(h, [(memv[:, :, CW * h + P * e:CW * h + P * e + P], e, 0) for e in range(2)], [2 * h, 2 * h + 1])
                     for h in range(4)], 0.0625)

        def order(s):
            c = Counts()

            def span(*names):
                return [i for name in names for i in range(lin[name].u0, lin[name].u1)]

            def project(*names):
                s.project(span(*names))

            def rms(gain=None):
                s.rms(c.norm, gain is not None and wants_column[c.gen - 1])
                c.norm += 1

            def residual(name, scale, gain):
                s.residual(c, name, scale, None if gain is None else GC[gain])
                c.gen += 1

            def head(src, nb, per, gain, before=(), after=()):
                s.head_norm(c, src, nb, per, gain, before, after)
                c.head += 1

            def att(kind, between=(), final=False):
                items, pvs, scale = attention(kind)
                s.attend(c, items, pvs, scale, between, final)
                c.att += len(items)
                c.pv += len(pvs)
                c.group += sum(1 for _, _, out in pvs if out)

            def mean(nb, per, gate, before=()):
                s.mean_norm(c, nb, per, gate, before)
                c.mean += 1
                c.meanb += nb

            def split_cat(a, b):
                s.cat_split(c, range(a, b))

            def rotate(src, perm, cs, sn, between=()):
                s.rotate(c, src, perm, cs, sn, between)
                c.rot += 4

            s.setup()
            s.first_fill(GC["ln00"])
            c.gen += 1
            for n in range(2):
                rms("x")
                s.ffn_up(2 * n, n, c, GC[f"ln{n}3"])
                c.norm += 1
                c.fill += 1
                residual(f"down{2 * n}", 0.5, f"ln{n}1")
                rms("x")
                memk = span(f"memk{n}")
                if n == 0:
                    project("aq", "ak", "av", "af")
                    s.forget_gates(c)
                    head(work[:, 16:24, :], 8, 64, ["even"] * 4 + [("even", 1)] * 4, memk[0:4], memk[4:8])
                    att("A", span("bq", "bk"))
                    memv = span("memv0")
                    head(work[:, 24:32, :], 8, 64, [("even", 2)] * 4 + [("even", 3)] * 4, span("bv"), memv[0:4])
                    rotate(work[:, 24:32, :], perm_rope, rope_c, rope_s, memv[4:8])
                    split_cat(0, 4)
                    att("B")
                    head(cat[:, 4:8, :], 4, 128, ["subln"] * 4)
                    split_cat(4, 8)
                else:
                    project("dq", "dk", "dv")
                    head(work[:, 16:24, :], 8, 64, ["odd"] * 4 + [("odd", 1)] * 4, memk[0:4], memk[4:8])
                    s.band_bias(c)
                    att("D", span("cb", "cc", "ch"))
                    s.conv(span("memv1"))
                    c.conv += 1
                    split_cat(0, 8)
                c.fill += 1
                residual(f"mixout{n}", 1.0, f"ln{n}2")
                rms("x")
                xq = span(f"xq{n}")
                head(memk_out, 8, 256, [(f"x{n}", 2 + b % 2) for b in range(8)], xq[0:4], xq[4:6])
                head(work[:, 16:20, :], 4, 256, [(f"x{n}", b % 2) for b in range(4)], xq[6:8])
                head(work[:, 20:24, :], 4, 256, [(f"x{n}", b % 2) for b in range(4)])
                att("X", final=True)
                c.fill += 1
                residual(f"xo{n}", 1.0, f"ln{n}4")
                rms("x")
                s.ffn_up(2 * n + 1, None, c, None)
                residual(f"down{2 * n + 1}", 0.5, f"ln{n + 1}0" if n == 0 else "pre0")
            for n in range(2):
                rms("x")
                s.ffn_up(4 + 2 * n, None, c, None)
                residual(f"down{4 + 2 * n}", 0.5, f"mix{n}")
                rms("x")
                if n == 0:
                    project("rq", "rk")
                    rotate(work[:, 16:24, :], perm_ret, ret_c, ret_sn, span("rv"))
                    s.retention(span("rg"))
                    mean(4, 1, work[:, 24:28, :], span("eq"))
                    split_cat(0, 4)
                    project("ek")
                    rotate(work[:, 28:36, :], perm_rope, dil_c, dil_sn, span("ev"))
                    att("E", final=True)
                else:
                    project("ga", "gq")
                    s.gla_gates(span("gk"))
                    s.gla_scores(span("gv"))
                    gr = span("gr")
                    s.gla_outputs(gr[0:4])
                    mean(8, 2, work[:, 24:32, :], gr[4:8])
                    split_cat(0, 8)
                c.fill += 1
                residual(f"mixout{2 + n}", 1.0, f"post{n}")
                rms("x")
                s.ffn_up(5 + 2 * n, None, c, None)
                residual(f"down{5 + 2 * n}", 0.5, "pre1" if n == 0 else None)
            rms()
            s.write_out(GC["final"])

        def gain_col(g):
            name, i = g if isinstance(g, tuple) else (g, 0)
            return gains[:, GC[name] + i:GC[name] + i + 1]

        def out_ap(o):
            return acc[:, o % BANKS, 0:T]

        def wait_free(eng, o):
            if o >= BANKS:
                kind, n = freed[o - BANKS]
                eng.wait_ge((gate_evac, hid_mul, out_evac)[kind], n)

        name_of = {i: name for name, l in lin.items() for i in range(l.u0, l.u1)}

        def dest_ap(i):
            name, u = name_of[i], units[i]
            n = u.out - lin[name].o0
            if u.mode == "F":
                return work[:, dest[name] + n, :]
            return vals(dest[name], nblk[name])[:, u.half, CW * (n // 2):CW * (n // 2) + CW]

        def next_of(weave, done, step, steps):
            n = len(weave) * (step + 1) // steps
            return n + 1 if n < len(weave) and units[weave[n]].mode == "T" and units[weave[n]].half else n

        wants_column = [any(u.mode == "T" and u.src == "hn" and u.need == g for u in units) for g in range(14)]
        rcol = small[:, 46:48]
        g_q, g_k, g_v = work[:, 16:20, :], work[:, 20:24, :], vals(32, 8)
        g_kdec, g_kdecT = t1[:, 0:4, :], t1[:, 4:8, :]
        g_scores = prob[:, 0:2, :, :].rearrange("p s a t -> p (s a t)").rearrange("p (h n q) -> p h n q", h=4, n=4)
        carry = keep[:, 8:12, :]
        g_state = work[:, 4:16, :].rearrange("p (n h) e -> p n h e", n=3)
        g_decay = small[:, 0:16]
        nmax = small[:, 16:22].rearrange("p (s q) -> p s q", s=3)
        rsum = small[:, 22:28].rearrange("p (s q) -> p s q", s=3)
        rinv = small[:, 28:34].rearrange("p (s q) -> p s q", s=3)
        rinv_lam = small[:, 34:36]
        lam_sum, lam_exp, neg_lam = small[:, 40:42], small[:, 42:44], small[:, 44:45]

        fills = {"hn": (hn_hi, hn_lo, hn_hi_ready, hn_lo_ready), "mn": (mn_hi, mn_lo, mn_hi_ready, mn_lo_ready)}

        def forget_z(i):
            return t2[0:8, 2 + i, :]

        block = ctx.enter_context(nc.Block())

        @block.sync
        def _(sp):
            sp.dma_start(gains[:, :], io["gains"]).then_inc(const_in, 16)
            sp.dma_start(x[:, :, :], io["x"].rearrange("(k p) t -> p k t", p=P)).then_inc(x_in, 16)
            for r, (src, nk, width) in enumerate(loads):
                if r == 1:
                    sp.dma_start(mats[:, :, :], io["mats"]).then_inc(mats_in, 16)
                    sp.dma_start(colc[:, :], io["cols"]).then_inc(mats_in, 16)
                if r >= RING:
                    sp.wait_ge(w_lo_ready, last_of_load[r - RING] + 1)
                sp.dma_start(raw[:, r % RING, 0:nk, 0:width], src).then_inc(raw_in[r % RING], 16)
            for k in range(0, KB, 2):
                sp.wait_ge(normed, KB * MEM_NORMS + k + 2)
                sp.dma_start(out.rearrange("(k p) t -> p k t", p=P)[:, k:k + 2, :], t1[:, k:k + 2, :]).then_inc(final_out, 16)
            sp.wait_ge(final_out, 16 * KB // 2)

        @block.tensor
        def _(pe):
            s = Stages()
            state = Progress()

            def unit(i):
                u = units[i]
                if u.first:
                    wait_free(pe, u.out)
                pe.wait_ge(w_hi_ready, i + 1)
                if u.src == "hid":
                    a_hi, a_lo = hid_hi, hid_lo
                    pe.wait_ge(hid_hi_ready, u.need)
                    pe.wait_ge(hid_lo_ready, u.need)
                else:
                    a_hi, a_lo, r_hi, r_lo = fills[u.src]
                fresh = u.src != "hid" and (i == 0 or (units[i - 1].src, units[i - 1].need) != (u.src, u.need))
                if u.mode == "F":
                    wh, wl = w_hi[:, u.slot], w_lo[:, u.slot]
                    bank = out_ap(u.out)
                    for j in range(u.nk):
                        if fresh:
                            pe.wait_ge(r_hi, 8 * u.need + j + 1)
                            pe.wait_ge(r_lo, 8 * u.need + j + 1)
                        nc.tensor.matmul(bank, wh[:, j, :], a_hi[:, u.k0 + j, :], start=u.first and j == 0, stop=False)
                        nc.tensor.matmul(bank, wh[:, j, :], a_lo[:, u.k0 + j, :], start=False, stop=False)
                    pe.wait_ge(w_lo_ready, i + 1)
                    for j in range(u.nk):
                        mm = nc.tensor.matmul(bank, wl[:, j, :], a_hi[:, u.k0 + j, :], start=False,
                                              stop=u.last and j == u.nk - 1)
                else:
                    if fresh:
                        pe.wait_ge(r_hi, 8 * u.need + 8)
                        pe.wait_ge(r_lo, 8 * u.need + 8)
                    pair, t = u.slot - u.half, u.half
                    pe.wait_ge(w_hi_ready, i - u.half + 2)
                    pe.wait_ge(w_lo_ready, i - u.half + 2)
                    bank = out_ap(u.out).rearrange("p (s n) -> p s n", s=2)
                    for j in range(u.nk):
                        ah, al = a_hi[:, j, P * t:P * t + P], a_lo[:, j, P * t:P * t + P]
                        wh, wl = w_hi[:, pair:pair + 2, j, :], w_lo[:, pair:pair + 2, j, :]
                        nc.tensor.matmul(bank, ah, wh, start=j == 0, stop=False)
                        nc.tensor.matmul(bank, ah, wl, start=False, stop=False)
                        mm = nc.tensor.matmul(bank, al, wh, start=False, stop=j == u.nk - 1)
                mm.then_inc(unit_done, 1)
                if state.sums is not None and u.src == "hn" and i >= BANKS - 1:
                    sum_squares()

            def take(ids):
                for i in ids:
                    unit(i)
                    if units[i].last:
                        state.evac = freed[units[i].out][1]

            def sum_squares():
                i, column = state.sums
                state.sums = None
                pe.wait_ge(squares_added, 7 * (i + 1))
                mm = nc.tensor.matmul(wide[:, 0, 0:T], ones, t1[:, 0, :], start=True, stop=True)
                if column:
                    for t in range(2):
                        mm = nc.tensor.matmul(wide[:, 1, 2 * t:2 * t + 2], t1[:, 0, P * t:P * t + P], ones[:, 0:2],
                                              start=True, stop=True)
                mm.then_inc(sums_done, 1)

            def setup():
                pe.wait_ge(mats_in, 32)

            def rms(i, column):
                state.sums = (i, column)

            def write_out(gain):
                sum_squares()

            def residual(c, name, scale, gain):
                take(range(lin[name].u0, lin[name].u1))

            def ffn_up(f, n, c, gain):
                l = lin[f"up{f}"]
                for j, i in enumerate(range(l.u0, l.u1)):
                    unit(i)
                    if n is not None and j == 11:
                        pe.wait_ge(squares_added, 7 * (c.norm + 1))
                        nc.tensor.matmul(wide[:, 1, 0:T], ones, t1[:, 0, :], start=True, stop=True).then_inc(sums_done, 1)

            def head_norm(c, src, nb, per, gain, before, after):
                take(before)
                pe.wait_ge(head_sq, c.head + 1)
                if per == 256:
                    for h in range(nb // 2):
                        for e in range(2):
                            mm = nc.tensor.matmul(wide[:, h, 0:T], ones, t1[:, 2 * h + e, :], start=e == 0, stop=e == 1)
                else:
                    m = ones64 if per == 64 else ones
                    for b in range(nb // 2):
                        mm = nc.tensor.matmul(wide[:, b, :], m, t1[:, 2 * b:2 * b + 2, :].rearrange("p b t -> p (b t)"),
                                              start=True, stop=True)
                mm.then_inc(head_sums, 1)
                take(after)

            def rotate(c, src, perm, cs, sn, between):
                if c.rot == 0:
                    pe.wait_ge(head_normed, c.head)
                else:
                    pe.wait_ge(out_evac, state.evac)
                if c.mean:
                    pe.wait_ge(mean_act, 6 * c.mean)
                for b in range(4):
                    pe_rot = nc.tensor.matmul(wide[:, b, :], perm, src[:, 2 * b:2 * b + 2, :].rearrange("p b t -> p (b t)"),
                                              start=True, stop=True)
                    pe_rot.then_inc(rot_done, 1)
                take(between)

            def attend(c, items, pvs, scale, between, final):
                pv_of = {it: n for n, (it, _, _) in enumerate(pvs)}
                two_norms = scale == 0.0625
                pe.wait_ge(head_std, c.head)
                pe.wait_ge(head_normed, c.head - two_norms)
                if c.rot:
                    pe.wait_ge(rot_added, c.rot)
                if c.mean:
                    pe.wait_ge(mean_act, 6 * c.mean)
                if items[0][3] is not None:
                    pe.wait_ge(gate_step, 4)
                group, fresh, taken = c.group, True, 0
                for i in range(len(items) + 3):
                    if i < len(items):
                        q, k, bias, gate, _ = items[i]
                        if two_norms and i == 2:
                            pe.wait_ge(head_normed, c.head)
                        if i >= 2:
                            pe.wait_ge(biased, c.att + i - 1)
                        for t in range(2):
                            o = wide[:, i % 2, T * t:T * t + T]
                            for e in range(len(q)):
                                mm = nc.tensor.matmul(o, q[e][:, P * t:P * t + P], k[e],
                                                      start=e == 0, stop=e == len(q) - 1 and gate is None)
                            if gate is not None:
                                row = ident[0:8, gate:gate + 1]
                                nc.tensor.matmul(o, cum[:, P * t:P * t + P], row.to_broadcast([8, T]), start=False, stop=False)
                                mm = nc.tensor.matmul(o, row.to_broadcast([8, P]), ncum, start=False, stop=True)
                        mm.then_inc(scores, 1)
                    if i - 2 in pv_of:
                        n = pv_of[i - 2]
                        pe.wait_ge(probs, c.att + i - 1)
                        if c.pv + n:
                            pe.wait_ge(turned_copied, c.pv + n)
                        p = prob[:, (c.att + i - 2) % 3]
                        for kt in range(2):
                            for qt in range(2):
                                mm = nc.tensor.transpose(wide[:, 2, T * kt + P * qt:T * kt + P * qt + P],
                                                         p[:, qt, P * kt:P * kt + P], ident)
                        mm.then_inc(turned, 1)
                    if i - 3 in pv_of:
                        n = pv_of[i - 3]
                        pe.wait_ge(turned_copied, c.pv + n + 1)
                        if fresh and group:
                            pe.wait_ge(att_out, group)
                        for v, e, p0 in pvs[n][1]:
                            m = v.shape[2]
                            for kt in range(2):
                                mm = nc.tensor.matmul(wide[p0:p0 + m, 3, T * e:T * e + T], v[:, kt, :], probT[:, n % 2, kt, :],
                                                      start=kt == 0, stop=kt == 1)
                        mm.then_inc(attended, 1)
                        fresh = bool(pvs[n][2])
                        group += fresh
                    upto = next_of(between, taken, i, len(items) + 3)
                    take(between[taken:upto])
                    taken = upto

            def band_bias(c):
                pe.wait_ge(band_in, 16 * 9)
                pe.wait_ge(head_std, c.head)
                for h in range(8):
                    if h >= 4:
                        pe.wait_ge(band_masked, h - 3)
                    nc.tensor.matmul(wide[:, h % 4, :], reverse, band(h).rearrange("p q k -> p (q k)"), start=True, stop=True)\
                        .then_inc(band_turned, 1)
                pe.wait_ge(band_masked, 8)

            def retention(between):
                pe.wait_ge(rot_added, 8)
                pe.wait_ge(out_evac, state.evac)
                v, taken = vals(36, 4), 0
                for h in range(5):
                    if h < 4:
                        if h >= 2:
                            pe.wait_ge(ret_p, h - 1)
                        for kt in range(2):
                            mm = nc.tensor.matmul(wide[:, h % 2, T * kt:T * kt + T], work[:, 20 + h, P * kt:P * kt + P],
                                                  work[:, 16 + h, :], start=True, stop=True)
                        mm.then_inc(ret_s, 1)
                    if h:
                        pe.wait_ge(ret_p, h)
                        if h >= 3:
                            pe.wait_ge(ret_copied, h - 2)
                        for kt in range(2):
                            mm = nc.tensor.matmul(wide[:, 2 + h % 2, 0:T], v[:, kt, P * (h - 1):P * h], probT[:, (h - 1) % 2, kt, :],
                                                  start=kt == 0, stop=kt == 1)
                        mm.then_inc(ret_o, 1)
                    upto = next_of(between, taken, h, 5)
                    take(between[taken:upto])
                    taken = upto

            def mean_norm(c, nb, per, gate, before):
                for step in range(2):
                    if step:
                        take(before)
                    elif c.mean == 0:
                        pe.wait_ge(ret_copied, 4)
                    else:
                        pe.wait_ge(gla_dve, 25)
                    src = cat if step == 0 else t1
                    for h in range(nb // per):
                        if step:
                            pe.wait_ge(mean_act, 6 * c.mean + h + 1)
                        for e in range(per):
                            mm = nc.tensor.matmul(wide[:, h, 0:T], ones, src[:, per * h + e, :], start=e == 0, stop=e == per - 1)
                    mm.then_inc(mean_sums, 1)

            def gla_gates(between):
                pe.wait_ge(wa_in, 16)
                pe.wait_ge(out_evac, freed[lin["gq"].o0][1])
                for h in range(4):
                    mm = nc.tensor.matmul(wide[:, h, 0:T], wa2[96:128, P * h:P * h + P], t2[96:128, 6, :], start=True, stop=True)
                mm.then_inc(gla_mm, 1)
                take(between)

            def gla_scores(between):
                take(between[0:4])
                pe.wait_ge(gla_dve, 4)
                for h in range(4):
                    for t in range(2):
                        mm = nc.tensor.transpose(wide[:, h // 2, T * (h % 2) + P * t:T * (h % 2) + P * t + P],
                                                 g_kdec[:, h, P * t:P * t + P], ident)
                mm.then_inc(gla_mm, 1)
                for h in range(4):
                    for n in range(4):
                        mm = nc.tensor.matmul(wide[64 * (n % 2):64 * (n % 2) + 64, 2, P * h + 64 * (n // 2):P * h + 64 * (n // 2) + 64],
                                              g_k[:, h, 64 * n:64 * n + 64], g_q[:, h, 64 * n:64 * n + 64], start=True, stop=True)
                mm.then_inc(gla_mm, 1)
                take(between[4:8])

            def gla_outputs(between):
                pe.wait_ge(out_evac, state.evac)
                pe.wait_ge(gla_act, 7)
                pe.wait_ge(gla_dve, 5)
                for n in range(3):
                    for h in range(4):
                        if n:
                            pe.wait_ge(gla_dve, 5 + 4 * (n - 1) + h + 1)
                        p0 = 64 * (n % 2)
                        mm = nc.tensor.matmul(wide[:, h, 0:T], g_kdecT[p0:p0 + 64, h, P * (n // 2):P * (n // 2) + P],
                                              g_v[p0:p0 + 64, n // 2, CW * h:CW * h + CW], start=True, stop=True)
                        mm.then_inc(gla_mm, 1)
                    take(between[n:n + 1])
                pe.wait_ge(gla_dve, 17)
                for b in range(8):
                    h, e = b // 2, b % 2
                    if b >= 4:
                        pe.wait_ge(gla_dve, 17 + b - 3)
                    for n in range(4):
                        o = wide[:, b % 4, 64 * n:64 * n + 64]
                        mm = nc.tensor.matmul(o, g_v[:, n // 2, CW * h + P * e:CW * h + P * e + P],
                                              g_scores[:, h, n, :], start=True, stop=n == 0)
                        if n:
                            mm = nc.tensor.matmul(o, g_state[:, n - 1, h, P * e:P * e + P], g_q[:, h, 64 * n:64 * n + 64],
                                                  start=False, stop=True)
                    mm.then_inc(gla_mm, 1)
                    if b == 3:
                        take(between[3:4])
            s.setup, s.rms, s.residual, s.ffn_up, s.project, s.write_out = setup, rms, residual, ffn_up, take, write_out
            s.band_bias, s.conv = band_bias, take
            s.first_fill = s.cat_split = s.forget_gates = lambda *a: None
            s.head_norm, s.rotate, s.attend = head_norm, rotate, attend
            s.retention, s.mean_norm = retention, mean_norm
            s.gla_gates, s.gla_scores, s.gla_outputs = gla_gates, gla_scores, gla_outputs
            order(s)

        @block.scalar
        def _(act):
            s = Stages()
            state = Progress()

            def link(ins):
                state.chain += 1
                ins.then_inc(act_chain, 1)
                act.wait_ge(act_chain, state.chain)

            def split_after(i):
                while state.split < len(units) and (units[state.split].free or 0) <= i + 1:
                    n, u = state.split, units[state.split]
                    act.wait_ge(raw_in[u.raw % RING], 16 * (u.raw // RING + 1))
                    if u.free is not None:
                        act.wait_ge(unit_done, u.free)
                    nc.scalar.activation(w_hi[:, u.slot, 0:u.nk, :], raw[:, u.raw % RING, 0:u.nk, P * u.half:P * u.half + P],
                                         ACT.Copy).then_inc(w_hi_ready, 1)
                    state.split = n + 1

            def take(ids):
                for i in ids:
                    if units[i].last:
                        state.evac = freed[units[i].out][1]
                    split_after(i)

            def logs():
                nc.scalar.preload_act_table_set("natural_log_exp_and_others")

            def rsqrt(out, mean_scale, sums, between):
                link(nc.scalar.activation(between, sums, ACT.Ln, scale=mean_scale, bias=eps_col))
                return nc.scalar.activation(out, between, ACT.Exp, scale=-0.5)

            def setup():
                act.wait_ge(const_in, 16)
                act.wait_ge(x_in, 16)

            def high(k, gain):
                nc.scalar.activation(hn_hi[:, k, :], x[:, k, :], ACT.Copy, scale=gains[:, gain + k:gain + k + 1])\
                    .then_inc(hn_hi_ready, 1)

            def square(k):
                nc.scalar.activation(t1[:, k, :], x[:, k, :], ACT.Square).then_inc(squares, 1)

            def first_fill(gain):
                for k in range(8):
                    high(k, gain)
                split_after(-1)
                for k in range(8):
                    square(k)
                act.wait_ge(mats_in, 32)
                act.wait_ge(lam_step, 1)
                nc.scalar.activation(lam_exp, lam_sum, ACT.Exp).then_inc(lam_step, 1)
                act.wait_ge(rope_step, 1)
                nc.scalar.activation(rope_s, hidf[:, 0:1, :], ACT.Sin).then_inc(rope_step, 1)
                nc.scalar.activation(hidf[:, 1:2, :], hidf[:, 0:1, :], ACT.Sin, scale=0.5).then_inc(rope_step, 1)

            def rms(i, column):
                logs()
                act.wait_ge(sums_done, i + 1)
                if column:
                    rsqrt(rcol, 1.0 / D, wide[:, 1, 0:4:2], small[:, 48:50])
                rsqrt(rstd[:, 0, :], 1.0 / D, wide[:, 0, 0:T], rstd[:, 1, :]).then_inc(std_done, 1)

            def residual(c, name, scale, gain):
                l = lin[name]
                act.wait_ge(unit_done, last_reader["hn", c.gen - 1] + 1)
                if c.fill:
                    act.wait_ge(mn_lo_ready, 8 * c.fill)
                for n in range(l.u0, l.u1):
                    u = units[n]
                    if n < l.u1 - 1:
                        split_after(n)
                    if u.last:
                        act.wait_ge(out_evac, freed[u.out][1])
                        if gain is not None:
                            high(u.out - l.o0, gain)
                        square(u.out - l.o0)
                split_after(l.u1 - 1)

            def ffn_up(f, n, c, gain):
                l = lin[f"up{f}"]
                if f:
                    act.wait_ge(unit_done, last_hid_reader[f - 1] + 1)
                for ch in range(FF // CW):
                    u0, m0 = l.u0 + 4 * ch, HB * f + 2 * ch
                    for h in range(2):
                        split_after(u0 + h)
                        act.wait_ge(gate_evac, m0 + h + 1)
                        nc.scalar.activation(silu_g[:, h, :], silu_g[:, h, :], ACT.Silu).then_inc(silu_done, 1)
                    for h in range(2):
                        split_after(u0 + 2 + h)
                        act.wait_ge(hid_mul, m0 + h + 1)
                        nc.scalar.activation(hid_hi[:, 2 * ch + h, :], hidf[:, h, :], ACT.Copy).then_inc(hid_hi_ready, 1)
                    if n is not None and ch == 1:
                        act.wait_ge(mem_in, 16 * (n + 1))
                        for k in range(8):
                            nc.scalar.activation(t1[:, k, :], keep[:, k, :], ACT.Square).then_inc(squares, 1)
                    if n is not None and ch == 3:
                        act.wait_ge(sums_done, c.norm + 1)
                        rsqrt(t2[:, 0, :], 1.0 / D, wide[:, 1, 0:T], t2[:, 1, :]).then_inc(std_done, 1)
                        if c.fill:
                            act.wait_ge(unit_done, last_reader["mn", c.fill - 1] + 1)
                        for k in range(8):
                            act.wait_ge(normed, 8 * n + k + 1)
                            nc.scalar.activation(mn_hi[:, k, :], t1[:, k, :], ACT.Copy).then_inc(mn_hi_ready, 1)

            def cat_split(c, blocks):
                if c.group:
                    act.wait_ge(att_out, c.group)
                act.wait_ge(head_normed, c.head)
                if c.conv:
                    act.wait_ge(conv_done, 4 * c.conv)
                act.wait_ge(unit_done, last_reader["mn", c.fill - 1] + 1)
                for k in blocks:
                    if c.mean:
                        act.wait_ge(mean_normed, c.meanb - len(blocks) + k + 1)
                    cat_split_blocks([k])

            def cat_split_blocks(blocks):
                for k in blocks:
                    nc.scalar.activation(mn_hi[:, k, :], cat[:, k, :], ACT.Copy).then_inc(mn_hi_ready, 1)

            def head_norm(c, src, nb, per, gain, before, after):
                act.wait_ge(out_evac, state.evac)
                act.wait_ge(gate_step, 4)
                if c.group:
                    act.wait_ge(att_out, c.group)
                if c.head:
                    act.wait_ge(head_normed, c.head)
                nc.scalar.activation(t1[:, 0:nb, :], src, ACT.Square).then_inc(head_sq, 1)
                take(before)
                logs()
                act.wait_ge(head_sums, c.head + 1)
                if per == 256:
                    o, i = t2[:, 0:nb // 2, :], wide[:, 0:nb // 2, 0:T]
                else:
                    o, i = t2[:, 0:nb, :].rearrange("p (b a) t -> p b (a t)", a=2), wide[:, 0:nb // 2, :]
                rsqrt(o, 1.0 / per, i, o).then_inc(head_std, 1)
                take(after)

            def attend(c, items, pvs, scale, between, final):
                pv_of, taken, group = {it: n for n, (it, _, _) in enumerate(pvs)}, 0, c.group
                if final:
                    act.wait_ge(unit_done, last_reader["mn", c.fill - 1] + 1)
                for i in range(len(items) + 3):
                    if i < len(items):
                        g = c.att + i
                        act.wait_ge(biased, g + 1)
                        for qt in range(2):
                            p = prob[:, g % 3, qt, :]
                            e = nc.scalar.activation(p, p, ACT.Exp, bias=nmax[:, g % 3, qt:qt + 1],
                                                     accum_out=rsum[:, g % 3, qt:qt + 1])
                        e.then_inc(expd, 1)
                    if i - 2 in pv_of:
                        n = pv_of[i - 2]
                        act.wait_ge(turned, c.pv + n + 1)
                        if n >= 2:
                            act.wait_ge(attended, c.pv + n - 1)
                        nc.scalar.activation(probT[:, n % 2, :, :], wide[:, 2, :].rearrange("p (k q) -> p k q", k=2),
                                             ACT.Copy).then_inc(turned_copied, 1)
                    if final and i - 3 in pv_of and pvs[pv_of[i - 3]][2]:
                        group += 1
                        act.wait_ge(att_out, group)
                        cat_split_blocks(pvs[pv_of[i - 3]][2])
                    upto = next_of(between, taken, i, len(items) + 3)
                    take(between[taken:upto])
                    taken = upto

            def forget_gates(c):
                logs()
                act.wait_ge(gate_step, 1)
                nc.scalar.activation(forget_z(2), forget_z(1), ACT.Exp, scale=-1.0).then_inc(gate_step, 1)
                act.wait_ge(gate_step, 2)
                nc.scalar.activation(forget_z(2), forget_z(2), ACT.Ln, bias=1.0).then_inc(gate_step, 1)

            def mean_norm(c, nb, per, gate, before):
                for h in range(4):
                    act.wait_ge(mean_off, c.meanb + per * (h + 1))
                    nc.scalar.activation(t1[:, per * h:per * (h + 1), :], cat[:, per * h:per * (h + 1), :], ACT.Square)\
                        .then_inc(mean_act, 1)
                if c.mean:
                    take(before)
                act.wait_ge(out_evac, state.evac)
                nc.scalar.activation(gate, gate, ACT.Silu).then_inc(mean_act, 1)
                if not c.mean:
                    take(before)
                logs()
                act.wait_ge(mean_sums, 2 * c.mean + 2)
                o = t2[:, 0:nb // per, :]
                rsqrt(o, 1.0 / (P * per), wide[:, 0:nb // per, 0:T], o).then_inc(mean_act, 1)

            def rotate(c, src, perm, cs, sn, between):
                take(between)

            def gla_gates(between):
                z, e, l = t1[:, 0:4, :], t1[:, 4:8, :], t1[:, 4:8, :]
                b = t2[:, 0:4, :]
                logs()
                act.wait_ge(gla_dve, 1)
                nc.scalar.activation(e, z, ACT.Exp, scale=-1.0).then_inc(gla_act, 1)
                act.wait_ge(gla_act, 1)
                nc.scalar.activation(l, e, ACT.Ln, bias=1.0).then_inc(gla_act, 1)
                take(between[0:2])
                act.wait_ge(gla_dve, 2)
                nc.scalar.activation(t1[:, 4:8, :], b, ACT.Exp, scale=1.0 / 16.0).then_inc(gla_act, 1)
                nc.scalar.activation(work[:, 4:8, :], b, ACT.Exp, scale=-1.0 / 16.0).then_inc(gla_act, 1)
                take(between[2:3])
                act.wait_ge(gla_dve, 3)
                nc.scalar.activation(work[:, 0:4, :], work[:, 0:4, :], ACT.Exp, scale=1.0 / 16.0).then_inc(gla_act, 1)
                last = b.rearrange("p h t -> p (h t)").rearrange("p (c j) -> p c j", j=64)[:, :, 63]
                nc.scalar.activation(g_decay, last, ACT.Exp, scale=1.0 / 16.0).then_inc(gla_act, 1)
                take(between[3:4])

            def gla_scores(between):
                take(between[0:4])
                act.wait_ge(gla_mm, 2)
                nc.scalar.activation(g_kdecT.rearrange("p (a b) t -> p a (b t)", a=2), wide[:, 0:2, :], ACT.Copy)\
                    .then_inc(gla_act, 1)
                take(between[4:8])

            s.setup, s.rms, s.residual, s.ffn_up, s.project, s.first_fill = setup, rms, residual, ffn_up, take, first_fill
            s.cat_split, s.head_norm, s.attend, s.forget_gates = cat_split, head_norm, attend, forget_gates
            s.mean_norm, s.gla_gates, s.gla_scores, s.rotate = mean_norm, gla_gates, gla_scores, rotate
            s.retention = s.conv = s.gla_outputs = take
            s.band_bias = s.write_out = lambda *a: None
            order(s)

        @block.vector
        def _(dve):
            s = Stages()
            state = Progress()

            def link(ins):
                state.chain += 1
                ins.then_inc(dve_chain, 1)
                dve.wait_ge(dve_chain, state.chain)

            def split_after(i):
                while state.split < len(units) and (units[state.split].free or 0) <= i + 1:
                    n, u = state.split, units[state.split]
                    dve.wait_ge(w_hi_ready, n + 1)
                    if u.free is not None:
                        dve.wait_ge(unit_done, u.free)
                    nc.vector.tensor_tensor(w_lo[:, u.slot, 0:u.nk, :], raw[:, u.raw % RING, 0:u.nk, P * u.half:P * u.half + P],
                                            w_hi[:, u.slot, 0:u.nk, :].bitcast(F32), ALU.subtract).then_inc(w_lo_ready, 1)
                    state.split = n + 1

            def take(ids):
                for i in ids:
                    u, name = units[i], name_of[i]
                    dve.wait_ge(unit_done, i + 1)
                    ps = out_ap(u.out)
                    if name == "af":
                        ins = nc.vector.tensor_tensor(forget_z(0), ps[0:8], rstd[0:8, 0, :], ALU.mult)
                    elif name == "ga":
                        ins = nc.vector.tensor_tensor(t2[96:128, 6, :], ps[96:128], rstd[96:128, 0, :], ALU.mult)
                    elif u.src == "mn":
                        ins = nc.vector.tensor_copy(dest_ap(i), ps)
                    elif u.mode == "F":
                        ins = nc.vector.tensor_tensor(dest_ap(i), ps, rstd[:, 0, :], ALU.mult)
                    else:
                        ins = nc.vector.tensor_scalar(dest_ap(i), ps, rcol[:, u.half:u.half + 1], None, ALU.mult)
                    ins.then_inc(out_evac, 1)
                    state.evac = freed[u.out][1]
                    split_after(i)

            def setup():
                dve.wait_ge(const_in, 16)
                dve.wait_ge(x_in, 16)
                link(nc.vector.tensor_scalar(gain_col("subln"), gain_col("subln"), 1.0 - LAMBDA_INIT, None, ALU.mult))

            def low(k, gen, gain):
                dve.wait_ge(hn_hi_ready, 8 * gen + k + 1)
                nc.vector.scalar_tensor_tensor(hn_lo[:, k, :], x[:, k, :], gains[:, gain + k:gain + k + 1],
                                               hn_hi[:, k, :].bitcast(F32), ALU.mult, ALU.subtract).then_inc(hn_lo_ready, 1)

            def first_fill(gain):
                for k in range(8):
                    low(k, 0, gain)
                split_after(-1)
                dve.wait_ge(mats_in, 32)
                dve.wait_ge(lam_in, 16)
                lp = prob[:, 0, 0, :].rearrange("p (a b d) -> p a b d", a=2, b=2)
                pr = prob[:, 1, 0, 0:128].rearrange("p (a d) -> p a d", a=2)
                link(nc.vector.tensor_tensor(pr, lp[:, :, 0, :], lp[:, :, 1, :], ALU.mult))
                nc.vector.tensor_reduce(lam_sum, pr, AX.X, ALU.add).then_inc(lam_step, 1)
                dve.wait_ge(pos_in, 16)
                a, n, m = hidf[:, 0, :], hidf[:, 1, :], silu_g[:, 0, :]
                link(nc.vector.tensor_copy(n, pos[:, :]))
                link(nc.vector.tensor_scalar(a, n, rope_freq, None, ALU.mult))
                link(nc.vector.tensor_scalar(n, a, 1.0 / TWO_PI, None, ALU.mult))
                link(nc.vector.tensor_scalar(n, n, ROUND, None, ALU.add))
                link(nc.vector.tensor_scalar(n, n, -ROUND, None, ALU.add))
                for part in TWO_PI_PARTS:
                    link(nc.vector.scalar_tensor_tensor(a, n, -part, a, ALU.mult, ALU.add))
                link(nc.vector.tensor_scalar(m, a, PI, -TWO_PI, ALU.is_gt, ALU.mult))
                link(nc.vector.tensor_tensor(a, a, m, ALU.add))
                link(nc.vector.tensor_scalar(m, a, -PI, TWO_PI, ALU.is_lt, ALU.mult))
                link(nc.vector.tensor_tensor(a, a, m, ALU.add))
                nc.vector.tensor_scalar(a, a, PI, -PI, ALU.min, ALU.max).then_inc(rope_step, 1)
                dve.wait_ge(lam_step, 2)
                link(nc.vector.tensor_tensor(neg_lam, lam_exp[:, 1:2], lam_exp[:, 0:1], ALU.subtract))
                link(nc.vector.tensor_scalar(neg_lam, neg_lam, -LAMBDA_INIT, None, ALU.add))
                dve.wait_ge(rope_step, 3)
                link(nc.vector.tensor_tensor(n, n, n, ALU.mult))
                link(nc.vector.tensor_scalar(rope_c, hidf[:, 1:2, :], -2.0, 1.0, ALU.mult, ALU.add))

            def rms(i, column):
                dve.wait_ge(std_done, i + 1)

            def write_out(gain):
                for k in range(8):
                    nc.vector.scalar_tensor_tensor(t1[:, k, :], x[:, k, :], gains[:, gain + k:gain + k + 1], rstd[:, 0, :],
                                                   ALU.mult, ALU.mult).then_inc(normed, 1)

            def cat_split(c, blocks):
                for k in blocks:
                    dve.wait_ge(mn_hi_ready, 8 * c.fill + k + 1)
                    nc.vector.tensor_tensor(mn_lo[:, k, :], cat[:, k, :], mn_hi[:, k, :].bitcast(F32), ALU.subtract)\
                        .then_inc(mn_lo_ready, 1)

            def residual(c, name, scale, gain):
                l, later = lin[name], []
                for n in range(l.u0, l.u1):
                    u = units[n]
                    if u.last:
                        k = u.out - l.o0
                        dve.wait_ge(unit_done, n + 1)
                        if u.src == "hid":
                            link(nc.vector.scalar_tensor_tensor(hidf[:, k % 2, :], out_ap(u.out), scale, rstd[:, 0, :],
                                                                ALU.mult, ALU.mult))
                            nc.vector.tensor_tensor(x[:, k, :], x[:, k, :], hidf[:, k % 2, :], ALU.add).then_inc(out_evac, 1)
                        else:
                            nc.vector.tensor_tensor(x[:, k, :], x[:, k, :], out_ap(u.out), ALU.add).then_inc(out_evac, 1)
                        if gain is not None:
                            later.append(k)
                    if n < l.u1 - 1:
                        split_after(n)
                    for k in later:
                        low(k, c.gen, gain)
                    later = []
                split_after(l.u1 - 1)
                dve.wait_ge(out_evac, freed[l.o1 - 1][1])

            def ffn_up(f, n, c, gain):
                l = lin[f"up{f}"]

                def scaled(h):
                    dve.wait_ge(unit_done, u0 + h + 1)
                    nc.vector.tensor_tensor(silu_g[:, h, :], out_ap(units[u0 + h].out), rstd[:, 0, :], ALU.mult)\
                        .then_inc(gate_evac, 1)

                def mul(h):
                    dve.wait_ge(unit_done, u0 + 2 + h + 1)
                    dve.wait_ge(silu_done, m0 + h + 1)
                    if m0:
                        dve.wait_ge(hid_hi_ready, m0 - 1 + h)
                        dve.wait_ge(hid_lo_ready, m0 - 1 + h)
                    nc.vector.tensor_tensor(hidf[:, h, :], silu_g[:, h, :], out_ap(units[u0 + 2 + h].out),
                                            ALU.mult).then_inc(hid_mul, 1)

                def low_hid(h):
                    dve.wait_ge(hid_hi_ready, m0 + h + 1)
                    dve.wait_ge(hid_mul, m0 + h + 1)
                    nc.vector.tensor_tensor(hid_lo[:, 2 * ch + h, :], hidf[:, h, :], hid_hi[:, 2 * ch + h, :].bitcast(F32),
                                            ALU.subtract).then_inc(hid_lo_ready, 1)

                for ch in range(FF // CW):
                    u0, m0 = l.u0 + 4 * ch, HB * f + 2 * ch
                    for h in range(2):
                        scaled(h)
                        split_after(u0 + h)
                    for h in range(2):
                        mul(h)
                        split_after(u0 + 2 + h)
                        low_hid(h)
                    if n is not None and ch == 3:
                        dve.wait_ge(std_done, c.norm + 1)

                        def mem_low(k):
                            dve.wait_ge(mn_hi_ready, 8 * c.fill + k + 1)
                            nc.vector.tensor_tensor(mn_lo[:, k, :], t1[:, k, :], mn_hi[:, k, :].bitcast(F32), ALU.subtract)\
                                .then_inc(mn_lo_ready, 1)

                        for k in range(9):
                            if k < 8:
                                nc.vector.scalar_tensor_tensor(t1[:, k, :], keep[:, k, :], gains[:, gain + k:gain + k + 1],
                                                               t2[:, 0, :], ALU.mult, ALU.mult).then_inc(normed, 1)
                            if k:
                                mem_low(k - 1)

            def head_norm(c, src, nb, per, gain, before, after):
                take(before)
                dve.wait_ge(head_std, c.head + 1)
                if not before:
                    dve.wait_ge(head_sq, c.head + 1)
                for b in range(nb):
                    r = t2[:, b // 2 if per == 256 else b, :]
                    ins = nc.vector.scalar_tensor_tensor(src[:, b, :], src[:, b, :], gain_col(gain[b]), r, ALU.mult, ALU.mult)
                ins.then_inc(head_normed, 1)
                take(after)

            def rotate(c, src, perm, cs, sn, between):
                if c.rot == 0:
                    dve.wait_ge(head_normed, c.head)
                else:
                    dve.wait_ge(tables_in, 16 * 3)
                    dve.wait_ge(out_evac, state.evac)
                for b in range(4):
                    pair = src[:, 2 * b:2 * b + 2, :]
                    dve.wait_ge(rot_done, c.rot + b + 1)
                    nc.vector.tensor_tensor(t1[:, 2 * b:2 * b + 2, :], wide[:, b, :].rearrange("p (a t) -> p a t", a=2),
                                            sn.to_broadcast([P, 2, T]), ALU.mult)
                    ins = nc.vector.tensor_tensor(pair, pair, cs.to_broadcast([P, 2, T]), ALU.mult)
                link(ins)
                for b in range(4):
                    pair = src[:, 2 * b:2 * b + 2, :]
                    nc.vector.tensor_tensor(pair, pair, t1[:, 2 * b:2 * b + 2, :], ALU.add).then_inc(rot_added, 1)
                take(between)

            def attend(c, items, pvs, scale, between, final):
                pv_of, taken = {it: n for n, (it, _, _) in enumerate(pvs)}, 0
                bias0 = items[0][2]
                if bias0 is not None:
                    dve.wait_ge(masks_in, 32)
                    if c.head == 7:
                        dve.wait_ge(band_masked, 8)
                for i in range(len(items) + 3):
                    if i < len(items):
                        g = c.att + i
                        bias = items[i][2]
                        dve.wait_ge(scores, g + 1)
                        if i - 3 in pv_of:
                            dve.wait_ge(turned, c.pv + pv_of[i - 3] + 1)
                        if i >= 2:
                            dve.wait_ge(probs, g - 1)
                        src = wide[:, i % 2, :].rearrange("p (q k) -> p q k", q=2)
                        if bias is None:
                            link(nc.vector.tensor_scalar(prob[:, g % 3, :, :], src, scale, None, ALU.mult))
                        else:
                            link(nc.vector.scalar_tensor_tensor(prob[:, g % 3, :, :], src, scale, bias, ALU.mult, ALU.add))
                        nc.vector.tensor_reduce(nmax[:, g % 3, :], prob[:, g % 3, :, :], AX.X, ALU.max, negate=True)\
                            .then_inc(biased, 1)
                    if 1 <= i <= len(items):
                        g = c.att + i - 1
                        partner = items[i - 1][4]
                        dve.wait_ge(expd, g + 1)
                        link(nc.vector.reciprocal(rinv[:, g % 3, :], rsum[:, g % 3, :]))
                        p = prob[:, g % 3, :, :]
                        if partner is None:
                            nc.vector.tensor_tensor(p, p, rinv[:, g % 3, :].unsqueeze(2).to_broadcast([P, 2, T]), ALU.mult)\
                                .then_inc(probs, 1)
                        else:
                            link(nc.vector.tensor_scalar(rinv_lam, rinv[:, g % 3, :], neg_lam, None, ALU.mult))
                            dve.wait_ge(probs, g)
                            for qt in range(2):
                                ins = nc.vector.scalar_tensor_tensor(p[:, qt, :], p[:, qt, :], rinv_lam[:, qt:qt + 1],
                                                                     prob[:, (g - 1) % 3, qt, :], ALU.mult, ALU.add)
                            ins.then_inc(probs, 1)
                    if i - 3 in pv_of and pvs[pv_of[i - 3]][2]:
                        n = pv_of[i - 3]
                        b = pvs[n][2]
                        dve.wait_ge(attended, c.pv + n + 1)
                        nc.vector.tensor_copy(cat[:, b[0]:b[-1] + 1, :],
                                              wide[:, 3, 0:T * len(b)].rearrange("p (b t) -> p b t", t=T)).then_inc(att_out, 1)
                        if final:
                            cat_split(c, b)
                    upto = next_of(between, taken, i, len(items) + 3)
                    take(between[taken:upto])
                    taken = upto

            def forget_gates(c):
                dve.wait_ge(out_evac, state.evac)
                z, a, e, f = (forget_z(i) for i in range(4))
                link(nc.vector.tensor_scalar(z, z, gain_col("fb")[0:8], None, ALU.add))
                link(nc.vector.tensor_scalar(a, z, -1.0, None, ALU.mult))
                nc.vector.tensor_tensor(a, a, z, ALU.max).then_inc(gate_step, 1)
                dve.wait_ge(gate_step, 3)
                link(nc.vector.scalar_tensor_tensor(f, z, 0.0, e, ALU.min, ALU.subtract))
                link(nc.vector.memset(a, 1.0))
                link(nc.vector.tensor_tensor_scan(z, a, f, 0.0, ALU.mult, ALU.add))
                nc.vector.tensor_scalar(cum, z, 8.0, None, ALU.mult)
                nc.vector.tensor_scalar(ncum, z, -8.0, None, ALU.mult).then_inc(gate_step, 1)

            def band_bias(c):
                for h in range(8):
                    dve.wait_ge(band_turned, h + 1)
                    for qt in range(2):
                        ins = nc.vector.tensor_tensor(band(h)[:, qt, :], wide[:, h % 4, T * (1 - qt):T * (1 - qt) + T],
                                                      chunked_odd[:, qt, :], ALU.add)
                    ins.then_inc(band_masked, 1)
            def conv(ids):
                cb, cc, ch, y = work[:, 24:28, :], work[:, 28:32, :], work[:, 32:36, :], t1[:, 0:4, :]
                w = gains[:, GC["conv"]:GC["conv"] + 12]
                dve.wait_ge(out_evac, state.evac)
                for b in range(4):
                    link(nc.vector.tensor_tensor(ch[:, b, :], cc[:, b, :], ch[:, b, :], ALU.mult))
                    link(nc.vector.tensor_scalar(y[:, b, :], ch[:, b, :], w[:, 8 + b:9 + b], None, ALU.mult))
                    for back in (1, 2):
                        j = 4 * (2 - back) + b
                        link(nc.vector.scalar_tensor_tensor(y[:, b, back:T], ch[:, b, 0:T - back], w[:, j:j + 1],
                                                            y[:, b, back:T], ALU.mult, ALU.add))
                    nc.vector.tensor_tensor(cat[:, b, :], cb[:, b, :], y[:, b, :], ALU.mult).then_inc(conv_done, 1)
                    take(ids[2 * b:2 * b + 2])

            def retention(between):
                taken = 0
                for h in range(5):
                    if h < 4:
                        dve.wait_ge(ret_s, h + 1)
                        if h >= 2:
                            dve.wait_ge(ret_o, h - 1)
                        nc.vector.tensor_tensor(probT[:, h % 2, :, :], wide[:, h % 2, :].rearrange("p (k q) -> p k q", k=2),
                                                decay[:, h, :, :], ALU.mult).then_inc(ret_p, 1)
                    if h:
                        dve.wait_ge(ret_o, h)
                        nc.vector.tensor_copy(cat[:, h - 1, :], wide[:, 2 + h % 2, 0:T]).then_inc(ret_copied, 1)
                    upto = next_of(between, taken, h, 5)
                    take(between[taken:upto])
                    taken = upto

            def mean_norm(c, nb, per, gate, before):
                dve.wait_ge(mean_sums, 2 * c.mean + 1)
                if c.mean == 0:
                    dve.wait_ge(ret_copied, 4)
                else:
                    dve.wait_ge(gla_dve, 25)
                for b in range(nb):
                    nc.vector.scalar_tensor_tensor(cat[:, b, :], wide[:, b // per, 0:T], -1.0 / (P * per), cat[:, b, :],
                                                   ALU.mult, ALU.add).then_inc(mean_off, 1)
                if c.mean:
                    take(before)
                dve.wait_ge(mean_act, 6 * c.mean + 5)
                link(nc.vector.tensor_tensor(cat[:, 0:nb, :], cat[:, 0:nb, :], gate, ALU.mult))
                if not c.mean:
                    take(before)
                dve.wait_ge(mean_act, 6 * c.mean + 6)
                for b in range(nb):
                    nc.vector.tensor_tensor(cat[:, b, :], cat[:, b, :], t2[:, b // per, :], ALU.mult).then_inc(mean_normed, 1)

            def gla_gates(between):
                dve.wait_ge(gla_mm, 1)
                z, a, l, b = work[:, 0:4, :], t1[:, 0:4, :], t1[:, 4:8, :], t2[:, 0:4, :]
                flat = lambda v: v.rearrange("p h t -> p (h t)")
                for h in range(4):
                    ins = nc.vector.tensor_scalar(z[:, h, :], wide[:, h, 0:T], gain_col(("ba", h)), None, ALU.add)
                link(ins)
                link(nc.vector.tensor_scalar(a, z, -1.0, None, ALU.mult))
                nc.vector.tensor_tensor(a, a, z, ALU.max).then_inc(gla_dve, 1)
                take(between[0:2])
                dve.wait_ge(gla_act, 2)
                link(nc.vector.scalar_tensor_tensor(flat(z), flat(z), 0.0, flat(l), ALU.min, ALU.subtract))
                dve.wait_ge(pool_chain, 3)
                nc.vector.tensor_tensor_scan(flat(b), flat(carry), flat(z), 0.0, ALU.mult, ALU.add).then_inc(gla_dve, 1)
                take(between[2:3])
                dve.wait_ge(gla_dve, 2)
                chunks = flat(b).rearrange("p (c j) -> p c j", j=64)
                nc.vector.tensor_tensor(flat(z).rearrange("p (c j) -> p c j", j=64), chunks[:, :, 63:64].to_broadcast([P, 16, 64]),
                                        chunks, ALU.subtract).then_inc(gla_dve, 1)
                take(between[3:4])

            def gla_scores(between):
                dve.wait_ge(out_evac, state.evac)
                dve.wait_ge(gla_act, 6)
                flat = lambda v: v.rearrange("p h t -> p (h t)")
                nc.vector.scalar_tensor_tensor(flat(g_q), flat(g_q), float(P) ** -0.5, flat(t1[:, 4:8, :]), ALU.mult, ALU.mult)
                take(between[0:1])
                link(nc.vector.tensor_tensor(g_kdec, g_k, work[:, 0:4, :], ALU.mult))
                take(between[1:2])
                nc.vector.tensor_tensor(g_k, g_k, work[:, 4:8, :], ALU.mult).then_inc(gla_dve, 1)
                take(between[2:4])
                dve.wait_ge(pool_chain, 4)
                dve.wait_ge(gla_mm, 3)
                for r in range(2):
                    rows = slice(64 * r, 64 * r + 64)
                    ins = nc.vector.tensor_tensor(g_scores[rows, :, r::2, :].rearrange("p h c q -> p (h c) q"),
                                                  wide[rows, 2, :].rearrange("p (a q) -> p a q", q=64),
                                                  key_before[rows].unsqueeze(1).to_broadcast([64, 8, 64]), ALU.mult)
                ins.then_inc(gla_dve, 1)
                take(between[4:8])

            def gla_outputs(between):
                for n in range(3):
                    for h in range(4):
                        dve.wait_ge(gla_mm, 4 + 4 * n + h)
                        if n == 0:
                            ins = nc.vector.tensor_copy(g_state[:, 0, h, :], wide[:, h, 0:T])
                        else:
                            dve.wait_ge(gla_dve, 5 + 4 * (n - 1) + h + 1)
                            ins = nc.vector.scalar_tensor_tensor(g_state[:, n, h, :], g_state[:, n - 1, h, :],
                                                                 g_decay[:, 4 * h + n:4 * h + n + 1], wide[:, h, 0:T],
                                                                 ALU.mult, ALU.add)
                        ins.then_inc(gla_dve, 1)
                    take(between[n:n + 1])
                for b in range(8):
                    dve.wait_ge(gla_mm, 16 + b)
                    nc.vector.tensor_copy(cat[:, b, :], wide[:, b % 4, 0:T]).then_inc(gla_dve, 1)
                    if b == 3:
                        take(between[3:4])
            s.setup, s.rms, s.residual, s.ffn_up, s.project, s.first_fill = setup, rms, residual, ffn_up, take, first_fill
            s.cat_split, s.head_norm, s.attend, s.forget_gates, s.write_out = cat_split, head_norm, attend, forget_gates, write_out
            s.rotate, s.conv, s.retention, s.mean_norm = rotate, conv, retention, mean_norm
            s.gla_gates, s.gla_scores, s.gla_outputs = gla_gates, gla_scores, gla_outputs
            s.band_bias = band_bias
            order(s)

        @block.gpsimd
        def _(pool):
            s = Stages()

            def add_squares(i):
                for k in range(1, 8):
                    pool.wait_ge(squares, 8 * i + k + 1)
                    if 7 * i + k > 1:
                        pool.wait_ge(squares_added, 7 * i + k - 1)
                    nc.gpsimd.tensor_tensor(t1[:, 0, :], t1[:, 0, :], t1[:, k, :], ALU.add).then_inc(squares_added, 1)

            def setup():
                pool.dma_start(prob[:, 0, 0, :], io["lam"].partition_broadcast(P)).then_inc(lam_in, 16)
                pool.dma_start(pos[:, :], io["positions"].partition_broadcast(P)).then_inc(pos_in, 16)
                pool.dma_start(keep[:, 0:8, :], io["mem"].rearrange("(k p) t -> p k t", p=P)).then_inc(mem_in, 16)
                pool.dma_start(causal, io["masks"][:, 0:2, :]).then_inc(masks_in, 16)
                pool.dma_start(chunked, io["masks"][:, 2:4, :]).then_inc(masks_in, 16)
                nc.gpsimd.memset(wa2[96:128, :], 0.0).then_inc(pool_chain, 1)
                pool.wait_ge(pool_chain, 1)
                pool.dma_start(wa2[112:128, :], io["wa2"]).then_inc(wa_in, 16)

            def first_fill(gain):
                add_squares(0)

            def ffn_up(f, n, c, gain):
                if f == 1:
                    pool.wait_ge(mn_lo_ready, 8 * c.fill)
                    pool.dma_start(keep[:, 0:8, :], io["mem"].rearrange("(k p) t -> p k t", p=P)).then_inc(mem_in, 16)
                if n is not None:
                    add_squares(c.norm)

            def residual(c, name, scale, gain):
                add_squares(c.norm)
                if name == "down2":
                    pool.wait_ge(unit_done, lin[name].u1)
                    pool.dma_start(chunked_odd, io["masks"][:, 2:4, :]).then_inc(band_in, 16)
                    for h in range(8):
                        b = io["band"]
                        skew = bass.AP(b.tensor, 512 * h, [[1, P], [P, 2], [1, T]])
                        pool.dma_start(band(h), skew).then_inc(band_in, 16)
                if name == "down4":
                    pool.wait_ge(unit_done, lin[name].u1)
                    pool.dma_start(work[:, 0:4, :], io["rotations"]).then_inc(tables_in, 16)
                    pool.dma_start(dil_bias, io["masks"][:, 4:6, :]).then_inc(tables_in, 16)
                    pool.dma_start(keep[:, 8:16, :], io["decay"]).then_inc(tables_in, 16)

            def gla_gates(between):
                nc.gpsimd.memset(carry, 1.0).then_inc(pool_chain, 1)
                pool.wait_ge(pool_chain, 2)
                nc.gpsimd.memset(carry.rearrange("p h t -> p (h t)").rearrange("p (c j) -> p c j", j=64)[:, :, 0:1], 0.0)\
                    .then_inc(pool_chain, 1)
                nc.gpsimd.memset(g_scores, 0.0).then_inc(pool_chain, 1)

            s.setup, s.first_fill, s.ffn_up, s.residual, s.gla_gates = setup, first_fill, ffn_up, residual, gla_gates
            s.rms = s.project = s.head_norm = s.attend = s.mean_norm = s.cat_split = s.rotate = lambda *a: None
            s.forget_gates = s.band_bias = s.conv = s.retention = s.gla_scores = s.gla_outputs = s.write_out = lambda *a: None
            order(s)


PI = float(np.float32(np.pi))
TWO_PI = 2.0 * float(np.pi)
TWO_PI_PARTS = (6.28125, 1014 * 2.0 ** -19, TWO_PI - 6.28125 - 1014 * 2.0 ** -19)
ROUND = 1.5 * 2.0 ** 23


def constants():
    f32 = np.float32
    p = np.arange(P)
    mats = np.zeros((P, 7, P), f32)
    mats[:, 0] = np.eye(P)
    mats[:, 1] = 1.0
    mats[:, 2] = (p[:, None] // 64) == (p[None, :] // 64)
    for m in range(P):
        if m % 64 < 8:
            mats[m + 8, 3, m] = -1.0
        elif m % 64 < 16:
            mats[m - 8, 3, m] = 1.0
        mats[(m + 64) % P, 4, m] = -1.0 if m < 64 else 1.0
    mats[:, 6] = np.eye(P)[::-1]
    mats[:, 5, 0:64] = (p[:, None] % 64) <= np.arange(64)[None, :]
    rope = f32(500000.0) ** (-np.arange(0, 16, 2, dtype=f32) / f32(16))
    cols = np.zeros((P, 4), f32)
    cols[:, 0] = EPS
    for m in range(P):
        if m % 64 < 16:
            cols[m, 1] = rope[m % 8]
    t = np.arange(T)
    q, k = t[:, None], t[None, :]
    off = f32(-1e30)
    count = ((q >= k) & (q - k <= 128)) * 1.0 + ((q >= k) & ((q - k) % 4 == 0)) + ((q >= k) & ((q - k) % 16 == 0))
    kinds = [np.where(q >= k, f32(0), off), np.where(q // 64 >= k // 64, f32(0), off),
             np.where(count > 0, np.log(np.maximum(count, 1.0)), off)]
    masks = np.concatenate([m.astype(f32).reshape(2, P, T).transpose(1, 0, 2) for m in kinds], axis=1)
    decay = np.zeros((P, 8, T), f32)
    for h in range(4):
        g = 1.0 - 2.0 ** (-5.0 - h)
        d = np.where(k >= q, g ** np.maximum(k - q, 0), 0.0) * P ** -0.5
        decay[:, 2 * h:2 * h + 2] = d.reshape(2, P, T).transpose(1, 0, 2)
    freq = f32(10000.0) ** (-np.linspace(0.0, 1.0, 64, dtype=f32))
    ret = t.astype(f32)[None, :] * freq[p % 64][:, None]
    dil = t.astype(f32)[None, :] * cols[:, 1:2]
    rot = np.stack([np.cos(ret), np.sin(ret), np.cos(dil), np.sin(dil)], axis=1).astype(f32)
    return {"mats": mats, "cols": cols, "masks": np.ascontiguousarray(masks), "decay": decay, "rotations": rot}


def lay_out(inputs):
    GC, NG = gain_columns()
    gains = np.zeros((P, NG), np.float32)

    def put(name, v):
        gains[:, GC[name]:GC[name] + v.shape[1]] = v

    def blocks(v):
        return v.reshape(-1, P).T

    def twice(v):
        return np.concatenate([v, v], axis=-1).T

    for l in range(2):
        for j in range(5):
            put(f"ln{l}{j}", blocks(inputs["ln_gains"][l, j]))
        put(f"pre{l}", blocks(inputs["ffn_pre_norm_2"][l]))
        put(f"mix{l}", blocks(inputs["mix_norm_2"][l]))
        put(f"post{l}", blocks(inputs["ffn_post_norm_2"][l]))
        put(f"x{l}", blocks(inputs["x_qk_gains"][l]))
    put("final", blocks(inputs["final_norm_2"]))
    put("even", twice(inputs["even_qk_gains"][0]))
    put("odd", twice(inputs["odd_qk_gains"][0]))
    put("subln", blocks(inputs["even_subln_gain"][0]))
    put("conv", blocks(inputs["odd_conv_w"][0]))
    put("ba", blocks(inputs["gla_b_a_2"][0]))
    gains[0:8, GC["fb"]] = inputs["even_f_bias"][0]
    rel = inputs["odd_rel_bias"][0][:, ::-1]
    band = np.concatenate([np.repeat(rel[:, 0:1], 127, axis=1), rel, np.repeat(rel[:, 256:257], 128, axis=1)], axis=1)
    return {"x": np.ascontiguousarray(inputs["x"][0].T), "mem": np.ascontiguousarray(inputs["mem"][0].T), "gains": gains,
            "positions": inputs["positions"], "lam": inputs["even_lambda"].reshape(1, 256),
            "wa2": inputs["gla_w_a2_2"][0],
            "band": np.ascontiguousarray(band)}


_WEIGHTS = ["ffn1_w_in", "ffn1_w_out", "ffn2_w_in", "ffn2_w_out", "even_w_in", "even_w_out", "odd_w_in", "odd_w_out",
            "x_w_q", "x_w_kv", "x_w_o", "ffn_pre_w_gate_2", "ffn_pre_w_up_2", "ffn_pre_w_down_2", "ab_w_in_2",
            "ab_w_out_2", "gla_w_in_2", "gla_w_out_2", "ffn_post_w_gate_2", "ffn_post_w_up_2", "ffn_post_w_down_2"]


def kernel(**inputs):
    import concourse.bacc as _bacc
    from concourse.bass_utils import run_bass_kernel_spmd as _run

    inputs = {k: np.asarray(v) for k, v in inputs.items()}
    arrays = {**lay_out(inputs), **constants(), **{n: inputs[n] for n in _WEIGHTS}}
    arrays = {f"in_{k}": np.ascontiguousarray(v) for k, v in arrays.items()}
    nc = _bacc.Bacc("TRN2", target_bir_lowering=False, num_devices=1)
    io = {k[3:]: nc.dram_tensor(k, a.shape, mybir.dt.from_np(a.dtype), kind="ExternalInput").ap() for k, a in arrays.items()}
    out = nc.dram_tensor("out", (D, T), F32, kind="ExternalOutput").ap()
    build(nc, io, out)
    r = _run(nc, [arrays], core_ids=[0])
    return np.ascontiguousarray(r.results[0]["out"].T)[None]
```
